# Optimizing a Trainium2 kernel written in Bass

```python
import math
import jax, jax.numpy as jnp
from jax import lax
import numpy as np

D_MODEL = 1024
BATCH = 1
SEQ = 256
DEPTH = 2

HG_HEADS = 4
HG_DK = 128
HG_DV = 128
HG_WIDTH = HG_HEADS * HG_DV
HG_CHUNK = 64
DA_HEADS = 4
DA_HEAD_DIM = 64
DA_V_DIM = 2 * DA_HEAD_DIM
DA_WIDTH = DA_HEADS * DA_V_DIM
Q_BLOCK = 128
D_FF = 2816
N_EXPERTS = 8
TOP_K = 2
D_FF_EXPERT = 3584
N_DENSE = (DEPTH + 1) // 2
N_MOE = DEPTH // 2
ADA_CHUNKS = 6
EPS = 1e-6
IN_SIZES = (HG_HEADS * HG_DK, HG_HEADS * HG_DK, HG_WIDTH, HG_WIDTH,
            DA_HEADS * 2 * DA_HEAD_DIM, DA_HEADS * 2 * DA_HEAD_DIM, DA_WIDTH,
            D_MODEL, D_MODEL)
D_IN = sum(IN_SIZES)


def rmsnorm(x, g):
    xf = x.astype(jnp.float32)
    y = xf * lax.rsqrt(jnp.mean(xf * xf, axis=-1, keepdims=True) + EPS)
    return y * g.astype(jnp.float32)

def split_points():
    return [int(v) for v in np.cumsum(np.array(IN_SIZES))[:-1]]

def alibi_slopes(n_heads):
    return jnp.asarray(2.0 ** (-8.0 * np.arange(1, n_heads + 1) / n_heads), dtype=jnp.float32)

def hgrn_lower_bounds(lb_logits):
    p = jax.nn.softmax(lb_logits.astype(jnp.float32), axis=0)
    cum = jnp.cumsum(p, axis=0)
    return cum - cum[0:1]

def hgrn2_chunk_scan(q, k, v, log_f):
    B, H, S, dk = q.shape
    dv = v.shape[-1]
    L = HG_CHUNK
    nc = S // L

    def to_chunks(t):
        return jnp.moveaxis(t.reshape(B, H, nc, L, t.shape[-1]), 2, 0)

    causal = jnp.tril(jnp.ones((L, L), dtype=bool))

    def step(state, inp):
        qb, kb, vb, gb = inp
        b = jnp.cumsum(gb, axis=2)
        o_inter = jnp.einsum('bhtk,bhkv->bhtv', qb * jnp.exp(b), state)
        rel = b[:, :, :, None, :] - b[:, :, None, :, :]
        decay = jnp.exp(jnp.where(causal[:, :, None], rel, -jnp.inf))
        scores = jnp.einsum('bhtk,bhsk,bhtsk->bhts', qb, kb, decay)
        o_intra = jnp.einsum('bhts,bhsv->bhtv', scores, vb)
        b_last = b[:, :, -1:, :]
        k_dec = kb * jnp.exp(b_last - b)
        new_state = jnp.exp(b_last[:, :, 0, :])[..., None] * state + jnp.einsum('bhsk,bhsv->bhkv', k_dec, vb)
        return new_state, o_inter + o_intra

    s0 = jnp.zeros((B, H, dk, dv), jnp.float32)
    _, o = lax.scan(step, s0, (to_chunks(q), to_chunks(k), to_chunks(v), to_chunks(log_f)))
    return jnp.moveaxis(o, 0, 2).reshape(B, H, S, dv)

def diff_attention(q, k, v, lam):
    B, H, _, S, d = q.shape
    dv = v.shape[-1]
    nb = S // Q_BLOCK
    scale = d ** -0.5
    slopes = alibi_slopes(H)
    kpos = jnp.arange(S)
    q_blocks = jnp.moveaxis(q.reshape(B, H, 2, nb, Q_BLOCK, d), 3, 0)

    def block(args):
        qb, bi = args
        qpos = bi * Q_BLOCK + jnp.arange(Q_BLOCK)
        dist = qpos[:, None] - kpos[None, :]
        s = jnp.einsum('bhcqd,bhcsd->bhcqs', qb, k) * scale
        s = s - slopes[None, :, None, None, None] * dist.astype(jnp.float32)
        s = jnp.where(dist >= 0, s, -jnp.inf)
        p = jax.nn.softmax(s, axis=-1)
        w = p[:, :, 0] - lam * p[:, :, 1]
        return jnp.einsum('bhqs,bhsv->bhqv', w, v)

    o = lax.map(block, (q_blocks, jnp.arange(nb)))
    return jnp.moveaxis(o, 0, 2).reshape(B, H, S, dv)

def token_mixer(h, layer, w_in, lb, hg_norm_g, qn_g, kn_g, lam_vecs, subln_g, w_pa, w_pb, w_o):
    B, S, _ = h.shape
    dt = h.dtype
    proj = h @ w_in
    hq, hf, hi, hg, dq, dk, dvv, ga, gb = jnp.split(proj, split_points(), axis=-1)

    def heads(t, d):
        return t.reshape(B, S, -1, d).transpose(0, 2, 1, 3).astype(jnp.float32)
    z = heads(hf, HG_DK)
    lbh = lb.reshape(HG_HEADS, 1, HG_DK)
    log_f = jnp.logaddexp(jnp.log(lbh), jnp.log1p(-lbh) + jax.nn.log_sigmoid(z))
    k_in = (1.0 - lbh) * jax.nn.sigmoid(-z)
    o_hg = hgrn2_chunk_scan(heads(hq, HG_DK), k_in, heads(hi, HG_DV), log_f)
    o_hg = rmsnorm(o_hg, hg_norm_g).transpose(0, 2, 1, 3).reshape(B, S, HG_WIDTH)
    o_hg = (o_hg * jax.nn.silu(hg.astype(jnp.float32))).astype(dt)

    q = dq.reshape(B, S, DA_HEADS, 2, DA_HEAD_DIM).transpose(0, 2, 3, 1, 4)
    k = dk.reshape(B, S, DA_HEADS, 2, DA_HEAD_DIM).transpose(0, 2, 3, 1, 4)
    v = dvv.reshape(B, S, DA_HEADS, DA_V_DIM).transpose(0, 2, 1, 3).astype(jnp.float32)
    q = rmsnorm(q, qn_g)
    k = rmsnorm(k, kn_g)
    lam_init = 0.8 - 0.6 * math.exp(-0.3 * layer)
    lv = lam_vecs.astype(jnp.float32)
    lam = jnp.exp(jnp.sum(lv[0] * lv[1])) - jnp.exp(jnp.sum(lv[2] * lv[3])) + lam_init
    o_da = diff_attention(q, k, v, lam)
    o_da = (rmsnorm(o_da, subln_g) * (1.0 - lam_init)).transpose(0, 2, 1, 3).reshape(B, S, DA_WIDTH).astype(dt)

    y = jax.nn.sigmoid(ga) * (o_hg @ w_pa) + jax.nn.sigmoid(gb) * (o_da @ w_pb)
    return y @ w_o

def swiglu(h, w1, w3, w2):
    return (jax.nn.silu(h @ w1) * (h @ w3)) @ w2

def moe_swiglu(h, router, w1, w3, w2):
    B, S, D = h.shape
    t = h.reshape(B * S, D)
    logits = (t @ router).astype(jnp.float32)
    vals, idx = lax.top_k(logits, TOP_K)
    wts = jax.nn.softmax(vals, axis=-1)
    comb = jnp.sum(jax.nn.one_hot(idx, N_EXPERTS, dtype=jnp.float32) * wts[..., None], axis=1)
    out = jnp.zeros_like(t)
    for e in range(N_EXPERTS):
        out = out + comb[:, e:e + 1].astype(t.dtype) * swiglu(t, w1[e], w3[e], w2[e])
    return out.reshape(B, S, D)

def first_inputs(seed: int = 0) -> dict:
    key = jax.random.key(seed)
    ks = jax.random.split(key, 24)
    f32 = jnp.float32
    D = D_MODEL

    def nrm(k, shape, scale):
        return jax.random.normal(k, shape, f32) * scale

    def gain(k, shape):
        return 1.0 + 0.05 * jax.random.normal(k, shape, f32)

    return {
        "x": nrm(ks[0], (BATCH, SEQ, D), 1.0),
        "c": nrm(ks[1], (BATCH, D), 1.0),
        "ada_w": nrm(ks[2], (DEPTH, D, ADA_CHUNKS * D), 0.5 * D ** -0.5),
        "ada_b": nrm(ks[3], (DEPTH, ADA_CHUNKS * D), 0.02),
        "norm_mix_g": gain(ks[4], (DEPTH, D)),
        "norm_ffn_g": gain(ks[5], (DEPTH, D)),
        "w_in": nrm(ks[6], (DEPTH, D, D_IN), D ** -0.5),
        "hgrn_lb_logits": nrm(ks[7], (DEPTH, HG_HEADS * HG_DK), 0.5),
        "hgrn_norm_g": gain(ks[8], (DEPTH, HG_DV)),
        "da_qnorm_g": gain(ks[9], (DEPTH, DA_HEAD_DIM)),
        "da_knorm_g": gain(ks[10], (DEPTH, DA_HEAD_DIM)),
        "da_lambda": nrm(ks[11], (DEPTH, 4, DA_HEAD_DIM), 0.1),
        "da_subln_g": gain(ks[12], (DEPTH, DA_V_DIM)),
        "w_branch_a": nrm(ks[13], (DEPTH, HG_WIDTH, D), HG_WIDTH ** -0.5),
        "w_branch_b": nrm(ks[14], (DEPTH, DA_WIDTH, D), DA_WIDTH ** -0.5),
        "w_out": nrm(ks[15], (DEPTH, D, D), D ** -0.5),
        "ffn_w1": nrm(ks[16], (N_DENSE, D, D_FF), D ** -0.5),
        "ffn_w3": nrm(ks[17], (N_DENSE, D, D_FF), D ** -0.5),
        "ffn_w2": nrm(ks[18], (N_DENSE, D_FF, D), D_FF ** -0.5),
        "moe_router": nrm(ks[19], (N_MOE, D, N_EXPERTS), D ** -0.5),
        "moe_w1": nrm(ks[20], (N_MOE, N_EXPERTS, D, D_FF_EXPERT), D ** -0.5),
        "moe_w3": nrm(ks[21], (N_MOE, N_EXPERTS, D, D_FF_EXPERT), D ** -0.5),
        "moe_w2": nrm(ks[22], (N_MOE, N_EXPERTS, D_FF_EXPERT, D), D_FF_EXPERT ** -0.5),
    }

def first_block(x, c, ada_w, ada_b, norm_mix_g, norm_ffn_g, w_in, hgrn_lb_logits, hgrn_norm_g,
              da_qnorm_g, da_knorm_g, da_lambda, da_subln_g, w_branch_a, w_branch_b, w_out,
              ffn_w1, ffn_w3, ffn_w2, moe_router, moe_w1, moe_w3, moe_w2):
    dt = x.dtype
    lb_all = hgrn_lower_bounds(hgrn_lb_logits)
    cs = jax.nn.silu(c)
    for l in range(DEPTH):
        ada = cs @ ada_w[l] + ada_b[l]
        sh1, sc1, g1, sh2, sc2, g2 = jnp.split(ada[:, None, :], ADA_CHUNKS, axis=-1)
        h = (rmsnorm(x, norm_mix_g[l]) * (1.0 + sc1) + sh1).astype(dt)
        x = x + g1 * token_mixer(h, l, w_in[l], lb_all[l], hgrn_norm_g[l], da_qnorm_g[l], da_knorm_g[l],
                                 da_lambda[l], da_subln_g[l], w_branch_a[l], w_branch_b[l], w_out[l])
        h = (rmsnorm(x, norm_ffn_g[l]) * (1.0 + sc2) + sh2).astype(dt)
        if l % 2 == 0:
            f = swiglu(h, ffn_w1[l // 2], ffn_w3[l // 2], ffn_w2[l // 2])
        else:
            f = moe_swiglu(h, moe_router[l // 2], moe_w1[l // 2], moe_w3[l // 2], moe_w2[l // 2])
        x = x + g2 * f
    return x


MLA_HEADS = 8
MLA_NOPE_DIM = 64
MLA_ROPE_DIM = 32
MLA_V_DIM = 64
MLA_Q_RANK = 384
MLA_KV_RANK = 256
MLA_QK_DIM = MLA_NOPE_DIM + MLA_ROPE_DIM
MOBA_HEADS = 8
MOBA_HEAD_DIM = 64
MOBA_WIDTH = MOBA_HEADS * MOBA_HEAD_DIM
MOBA_BLOCK = 256
MOBA_TOPK = 3
MOBA_Q_CHUNK = 16
CONV_CH = 512
CONV_WIDTH = 31
FFN_CONV_WIDTH = 3
ATTN_Q_BLOCK = 128
ROPE_THETA = 10000.0
NORM_EPS = 1e-6
N_BRANCH = 3
D_IN_2 = MLA_Q_RANK + MLA_KV_RANK + MLA_ROPE_DIM + 3 * MOBA_WIDTH + 2 * CONV_CH + N_BRANCH * D_MODEL


def rms_norm(x, g):
    xf = x.astype(jnp.float32)
    y = xf * lax.rsqrt(jnp.mean(xf * xf, axis=-1, keepdims=True) + NORM_EPS)
    return (y * g.astype(jnp.float32)).astype(x.dtype)

def layer_norm(x, g, b):
    xf = x.astype(jnp.float32)
    mu = jnp.mean(xf, axis=-1, keepdims=True)
    var = jnp.mean(jnp.square(xf - mu), axis=-1, keepdims=True)
    y = (xf - mu) * lax.rsqrt(var + NORM_EPS) * g.astype(jnp.float32) + b.astype(jnp.float32)
    return y.astype(x.dtype)

def rope_tables(positions, dim):
    inv_freq = 1.0 / (ROPE_THETA ** (jnp.arange(0, dim, 2, dtype=jnp.float32) / dim))
    ang = positions.astype(jnp.float32)[..., None] * inv_freq
    return jnp.cos(ang), jnp.sin(ang)

def apply_rope(x, cos, sin):
    xf = x.astype(jnp.float32)
    x1, x2 = jnp.split(xf, 2, axis=-1)
    c, s = cos[:, None], sin[:, None]
    return jnp.concatenate([x1 * c - x2 * s, x2 * c + x1 * s], axis=-1).astype(x.dtype)

def causal_depthwise_conv(x, w, b):
    width = w.shape[0]
    y = lax.conv_general_dilated(
        x, w[:, None, :].astype(x.dtype), window_strides=(1,), padding=[(width - 1, 0)],
        dimension_numbers=('NWC', 'WIO', 'NWC'), feature_group_count=x.shape[-1])
    return y + b

def modulate(h, shift, scale):
    return h * (1.0 + scale[:, None, :]) + shift[:, None, :]

def causal_attention(q, k, v):
    B, H, S, dqk = q.shape
    dv = v.shape[-1]
    nqb = S // ATTN_Q_BLOCK
    scale = dqk ** -0.5
    q_blocks = q.reshape(B, H, nqb, ATTN_Q_BLOCK, dqk).transpose(2, 0, 1, 3, 4)
    kpos = jnp.arange(S)

    def one_block(args):
        qb, bi = args
        s = jnp.einsum('bhqd,bhkd->bhqk', qb, k).astype(jnp.float32) * scale
        qpos = bi * ATTN_Q_BLOCK + jnp.arange(ATTN_Q_BLOCK)
        s = jnp.where(kpos[None, :] <= qpos[:, None], s, -jnp.inf)
        p = jax.nn.softmax(s, axis=-1).astype(v.dtype)
        return jnp.einsum('bhqk,bhkd->bhqd', p, v)

    o = lax.map(one_block, (q_blocks, jnp.arange(nqb)))
    return o.transpose(1, 2, 0, 3, 4).reshape(B, H, S, dv)

def moba_attention(q, k, v):
    B, H, S, d = q.shape
    nb = -(-S // MOBA_BLOCK)
    s_pad = nb * MOBA_BLOCK
    pad = [(0, 0), (0, 0), (0, s_pad - S), (0, 0)]
    q, k, v = jnp.pad(q, pad), jnp.pad(k, pad), jnp.pad(v, pad)
    k_blocks = k.reshape(B, H, nb, MOBA_BLOCK, d)
    v_blocks = v.reshape(B, H, nb, MOBA_BLOCK, d)
    k_mean = jnp.mean(k_blocks.astype(jnp.float32), axis=3)
    block_score = jnp.einsum('bhsd,bhnd->bhsn', q.astype(jnp.float32), k_mean)
    q_blk = jnp.arange(s_pad) // MOBA_BLOCK
    fully_past = jnp.arange(nb)[None, :] < q_blk[:, None]
    block_score = jnp.where(fully_past[None, None], block_score, -jnp.inf)
    topk = min(MOBA_TOPK, nb)
    _, sel = lax.top_k(block_score, topk)

    nc = s_pad // MOBA_Q_CHUNK
    q_c = q.reshape(B, H, nc, MOBA_Q_CHUNK, d).transpose(2, 0, 1, 3, 4)
    sel_c = sel.reshape(B, H, nc, MOBA_Q_CHUNK, topk).transpose(2, 0, 1, 3, 4)
    b_idx = jnp.arange(B)[:, None, None, None]
    h_idx = jnp.arange(H)[None, :, None, None]
    jpos = jnp.arange(MOBA_BLOCK)
    scale = d ** -0.5

    def one_chunk(args):
        qc, sc, ci = args
        qpos = ci * MOBA_Q_CHUNK + jnp.arange(MOBA_Q_CHUNK)
        own = (ci * MOBA_Q_CHUNK) // MOBA_BLOCK
        k_sel = k_blocks[b_idx, h_idx, sc]
        v_sel = v_blocks[b_idx, h_idx, sc]
        s_sel = jnp.einsum('bhqd,bhqnjd->bhqnj', qc, k_sel).astype(jnp.float32) * scale
        valid = jnp.arange(topk)[None, :] < (qpos // MOBA_BLOCK)[:, None]
        s_sel = jnp.where(valid[None, None, :, :, None], s_sel, -jnp.inf)
        k_own = lax.dynamic_index_in_dim(k_blocks, own, axis=2, keepdims=False)
        v_own = lax.dynamic_index_in_dim(v_blocks, own, axis=2, keepdims=False)
        s_own = jnp.einsum('bhqd,bhjd->bhqj', qc, k_own).astype(jnp.float32) * scale
        causal = own * MOBA_BLOCK + jpos[None, :] <= qpos[:, None]
        s_own = jnp.where(causal[None, None], s_own, -jnp.inf)
        s_all = jnp.concatenate([s_sel.reshape(B, H, MOBA_Q_CHUNK, topk * MOBA_BLOCK), s_own], axis=-1)
        p = jax.nn.softmax(s_all, axis=-1).astype(v.dtype)
        p_sel = p[..., :topk * MOBA_BLOCK].reshape(B, H, MOBA_Q_CHUNK, topk, MOBA_BLOCK)
        p_own = p[..., topk * MOBA_BLOCK:]
        return (jnp.einsum('bhqnj,bhqnjd->bhqd', p_sel, v_sel)
                + jnp.einsum('bhqj,bhjd->bhqd', p_own, v_own))

    o = lax.map(one_chunk, (q_c, sel_c, jnp.arange(nc)))
    return o.transpose(1, 2, 0, 3, 4).reshape(B, H, s_pad, d)[:, :, :S]

def token_mixer_2(h, cos_a, sin_a, cos_b, sin_b, w_in,
                mla_q_norm_g, w_uq, mla_kv_norm_g, w_ukv,
                mla_qn_nope_g, mla_qn_rope_g, mla_kn_nope_g, mla_kn_rope_g, w_mla_o,
                moba_qn_g, moba_kn_g, w_moba_o,
                conv_dw_w, conv_dw_b, conv_ln_g, conv_ln_b, w_conv_pw2, b_conv_pw2,
                w_out):
    B, S, _ = h.shape
    z = h @ w_in
    sizes = (MLA_Q_RANK, MLA_KV_RANK, MLA_ROPE_DIM, 3 * MOBA_WIDTH, 2 * CONV_CH, N_BRANCH * D_MODEL)
    q_lat, kv_lat, k_rope, qkv_b, conv_in, gate_logits = jnp.split(
        z, np.cumsum(sizes)[:-1].tolist(), axis=-1)

    q_a = (rms_norm(q_lat, mla_q_norm_g) @ w_uq).reshape(B, S, MLA_HEADS, MLA_QK_DIM).transpose(0, 2, 1, 3)
    q_nope = rms_norm(q_a[..., :MLA_NOPE_DIM], mla_qn_nope_g)
    q_pe = apply_rope(rms_norm(q_a[..., MLA_NOPE_DIM:], mla_qn_rope_g), cos_a, sin_a)
    kv = (rms_norm(kv_lat, mla_kv_norm_g) @ w_ukv).reshape(
        B, S, MLA_HEADS, MLA_NOPE_DIM + MLA_V_DIM).transpose(0, 2, 1, 3)
    k_nope = rms_norm(kv[..., :MLA_NOPE_DIM], mla_kn_nope_g)
    v_a = kv[..., MLA_NOPE_DIM:]
    k_pe = apply_rope(rms_norm(k_rope, mla_kn_rope_g)[:, None], cos_a, sin_a)
    q_full = jnp.concatenate([q_nope, q_pe], axis=-1)
    k_full = jnp.concatenate([k_nope, jnp.broadcast_to(k_pe, (B, MLA_HEADS, S, MLA_ROPE_DIM))], axis=-1)
    o_a = causal_attention(q_full, k_full, v_a)
    o_a = o_a.transpose(0, 2, 1, 3).reshape(B, S, MLA_HEADS * MLA_V_DIM) @ w_mla_o

    qkv = qkv_b.reshape(B, S, 3, MOBA_HEADS, MOBA_HEAD_DIM).transpose(2, 0, 3, 1, 4)
    q_b = apply_rope(rms_norm(qkv[0], moba_qn_g), cos_b, sin_b)
    k_b = apply_rope(rms_norm(qkv[1], moba_kn_g), cos_b, sin_b)
    o_b = moba_attention(q_b, k_b, qkv[2])
    o_b = o_b.transpose(0, 2, 1, 3).reshape(B, S, MOBA_WIDTH) @ w_moba_o

    glu_a, glu_g = jnp.split(conv_in, 2, axis=-1)
    u = glu_a * jax.nn.sigmoid(glu_g)
    u = causal_depthwise_conv(u, conv_dw_w, conv_dw_b)
    u = jax.nn.silu(layer_norm(u, conv_ln_g, conv_ln_b))
    o_c = u @ w_conv_pw2 + b_conv_pw2

    g = jax.nn.sigmoid(gate_logits.reshape(B, S, N_BRANCH, D_MODEL))
    merged = g[:, :, 0] * o_a + g[:, :, 1] * o_b + g[:, :, 2] * o_c
    return merged @ w_out

def channel_mixer(h, w_up, ffn_dw_w, ffn_dw_b, w_down):
    u = causal_depthwise_conv(h @ w_up, ffn_dw_w, ffn_dw_b)
    a, b = jnp.split(u, 2, axis=-1)
    return (jax.nn.silu(a) * b) @ w_down

def second_inputs(seed: int = 0) -> dict:
    key = jax.random.key(seed)
    ks = iter(jax.random.split(key, 48))
    L = DEPTH

    def nrm(shape, fan_in):
        return jax.random.normal(next(ks), shape, jnp.float32) * (fan_in ** -0.5)

    def gain(shape):
        return 1.0 + 0.02 * jax.random.normal(next(ks), shape, jnp.float32)

    def bias(shape):
        return 0.01 * jax.random.normal(next(ks), shape, jnp.float32)

    x = jax.random.normal(next(ks), (BATCH, SEQ, D_MODEL), jnp.float32)
    c = jax.random.normal(next(ks), (BATCH, D_MODEL), jnp.float32)
    offset = jax.random.randint(next(ks), (BATCH, 1), 0, 1024, dtype=jnp.int32)
    positions = (offset + jnp.arange(SEQ, dtype=jnp.int32)[None, :]).astype(jnp.int32)
    return {
        'x': x, 'c': c, 'positions': positions,
        'w_mod': nrm((L, D_MODEL, 6 * D_MODEL), D_MODEL), 'b_mod': bias((L, 6 * D_MODEL)),
        'mix_norm_g': gain((L, D_MODEL)), 'w_in': nrm((L, D_MODEL, D_IN_2), D_MODEL),
        'mla_q_norm_g': gain((L, MLA_Q_RANK)),
        'w_uq': nrm((L, MLA_Q_RANK, MLA_HEADS * MLA_QK_DIM), MLA_Q_RANK),
        'mla_kv_norm_g': gain((L, MLA_KV_RANK)),
        'w_ukv': nrm((L, MLA_KV_RANK, MLA_HEADS * (MLA_NOPE_DIM + MLA_V_DIM)), MLA_KV_RANK),
        'mla_qn_nope_g': gain((L, MLA_NOPE_DIM)), 'mla_qn_rope_g': gain((L, MLA_ROPE_DIM)),
        'mla_kn_nope_g': gain((L, MLA_NOPE_DIM)), 'mla_kn_rope_g': gain((L, MLA_ROPE_DIM)),
        'w_mla_o': nrm((L, MLA_HEADS * MLA_V_DIM, D_MODEL), MLA_HEADS * MLA_V_DIM),
        'moba_qn_g': gain((L, MOBA_HEAD_DIM)), 'moba_kn_g': gain((L, MOBA_HEAD_DIM)),
        'w_moba_o': nrm((L, MOBA_WIDTH, D_MODEL), MOBA_WIDTH),
        'conv_dw_w': nrm((L, CONV_WIDTH, CONV_CH), CONV_WIDTH), 'conv_dw_b': bias((L, CONV_CH)),
        'conv_ln_g': gain((L, CONV_CH)), 'conv_ln_b': bias((L, CONV_CH)),
        'w_conv_pw2': nrm((L, CONV_CH, D_MODEL), CONV_CH), 'b_conv_pw2': bias((L, D_MODEL)),
        'w_out': nrm((L, D_MODEL, D_MODEL), D_MODEL),
        'ffn_norm_g': gain((L, D_MODEL)), 'w_up': nrm((L, D_MODEL, 2 * D_FF), D_MODEL),
        'ffn_dw_w': nrm((L, FFN_CONV_WIDTH, 2 * D_FF), FFN_CONV_WIDTH), 'ffn_dw_b': bias((L, 2 * D_FF)),
        'w_down': nrm((L, D_FF, D_MODEL), D_FF),
    }

def second_block(x, c, positions, w_mod, b_mod, mix_norm_g, w_in,
              mla_q_norm_g, w_uq, mla_kv_norm_g, w_ukv,
              mla_qn_nope_g, mla_qn_rope_g, mla_kn_nope_g, mla_kn_rope_g, w_mla_o,
              moba_qn_g, moba_kn_g, w_moba_o,
              conv_dw_w, conv_dw_b, conv_ln_g, conv_ln_b, w_conv_pw2, b_conv_pw2,
              w_out, ffn_norm_g, w_up, ffn_dw_w, ffn_dw_b, w_down):
    cos_a, sin_a = rope_tables(positions, MLA_ROPE_DIM)
    cos_b, sin_b = rope_tables(positions, MOBA_HEAD_DIM)
    c_act = jax.nn.silu(c)
    for l in range(DEPTH):
        mod = c_act @ w_mod[l] + b_mod[l]
        sh1, sc1, g1, sh2, sc2, g2 = jnp.split(mod, 6, axis=-1)
        h = modulate(rms_norm(x, mix_norm_g[l]), sh1, sc1)
        y = token_mixer_2(h, cos_a, sin_a, cos_b, sin_b, w_in[l],
                        mla_q_norm_g[l], w_uq[l], mla_kv_norm_g[l], w_ukv[l],
                        mla_qn_nope_g[l], mla_qn_rope_g[l], mla_kn_nope_g[l], mla_kn_rope_g[l], w_mla_o[l],
                        moba_qn_g[l], moba_kn_g[l], w_moba_o[l],
                        conv_dw_w[l], conv_dw_b[l], conv_ln_g[l], conv_ln_b[l], w_conv_pw2[l], b_conv_pw2[l],
                        w_out[l])
        x = x + g1[:, None, :] * y
        h = modulate(rms_norm(x, ffn_norm_g[l]), sh2, sc2)
        x = x + g2[:, None, :] * channel_mixer(h, w_up[l], ffn_dw_w[l], ffn_dw_b[l], w_down[l])
    return x


def setup_inputs(seed=0):
    out = dict(first_inputs(seed))
    for name, value in second_inputs(seed + 1).items():
        if name != "x":
            out[name + "_2"] = value
    return out


def reference(
    x, c, ada_w, ada_b, norm_mix_g, norm_ffn_g, w_in, hgrn_lb_logits, hgrn_norm_g, da_qnorm_g,
    da_knorm_g, da_lambda, da_subln_g, w_branch_a, w_branch_b, w_out, ffn_w1, ffn_w3, ffn_w2,
    moe_router, moe_w1, moe_w3, moe_w2, c_2, positions_2, w_mod_2, b_mod_2, mix_norm_g_2,
    w_in_2, mla_q_norm_g_2, w_uq_2, mla_kv_norm_g_2, w_ukv_2, mla_qn_nope_g_2, mla_qn_rope_g_2,
    mla_kn_nope_g_2, mla_kn_rope_g_2, w_mla_o_2, moba_qn_g_2, moba_kn_g_2, w_moba_o_2,
    conv_dw_w_2, conv_dw_b_2, conv_ln_g_2, conv_ln_b_2, w_conv_pw2_2, b_conv_pw2_2, w_out_2,
    ffn_norm_g_2, w_up_2, ffn_dw_w_2, ffn_dw_b_2, w_down_2,
):
    x = first_block(
        x, c, ada_w, ada_b, norm_mix_g, norm_ffn_g, w_in, hgrn_lb_logits, hgrn_norm_g,
        da_qnorm_g, da_knorm_g, da_lambda, da_subln_g, w_branch_a, w_branch_b, w_out, ffn_w1,
        ffn_w3, ffn_w2, moe_router, moe_w1, moe_w3, moe_w2,
    )
    return second_block(
        x, c_2, positions_2, w_mod_2, b_mod_2, mix_norm_g_2, w_in_2, mla_q_norm_g_2, w_uq_2,
        mla_kv_norm_g_2, w_ukv_2, mla_qn_nope_g_2, mla_qn_rope_g_2, mla_kn_nope_g_2,
        mla_kn_rope_g_2, w_mla_o_2, moba_qn_g_2, moba_kn_g_2, w_moba_o_2, conv_dw_w_2,
        conv_dw_b_2, conv_ln_g_2, conv_ln_b_2, w_conv_pw2_2, b_conv_pw2_2, w_out_2,
        ffn_norm_g_2, w_up_2, ffn_dw_w_2, ffn_dw_b_2, w_down_2,
    )


_drawn_inputs = setup_inputs


def setup_inputs(seed=0):
    import zlib

    import numpy as np

    out = dict(_drawn_inputs(seed))
    spreads = {}
    factors = {'hgrn_norm_g': 4.047,
     'da_qnorm_g': 4.707,
     'da_knorm_g': 4.013,
     'da_subln_g': 4.055,
     'b_mod_2': 3.053,
     'mix_norm_g_2': 6.86,
     'mla_q_norm_g_2': 8.0,
     'mla_kv_norm_g_2': 8.0,
     'mla_qn_nope_g_2': 8.0,
     'mla_qn_rope_g_2': 8.0,
     'mla_kn_nope_g_2': 8.0,
     'mla_kn_rope_g_2': 8.0,
     'moba_qn_g_2': 8.0,
     'moba_kn_g_2': 8.0,
     'conv_dw_b_2': 8.0,
     'conv_ln_g_2': 8.0,
     'conv_ln_b_2': 8.0,
     'b_conv_pw2_2': 8.0,
     'ffn_norm_g_2': 3.091,
     'ffn_dw_b_2': 7.153}
    for name, (base, spread) in spreads.items():
        noise = np.random.default_rng([zlib.crc32(name.encode()), seed]).standard_normal(out[name].shape)
        drawn = base * np.exp(spread * noise) if base else spread * noise
        out[name] = __import__('jax').numpy.asarray(drawn.astype(out[name].dtype))
    for name, factor in factors.items():
        out[name] = (out[name] * factor).astype(out[name].dtype)
    return out
```

```python
from contextlib import ExitStack
import math

import numpy as np
import concourse.bass as bass
from concourse import mybir

ALU = mybir.AluOpType
ACT = mybir.ActivationFunctionType
F32 = mybir.dt.float32
I32 = mybir.dt.int32
AX = mybir.AxisListType

P = 128
T = 256
D = 1024
DK = D // P
EPS = 1e-6
D_FF = 2816
FF_U = D_FF // 256
D_FE = 3584
FE_U = D_FE // 256
EXPERTS = 8
CONV_W = 31
RING = 4
SLOT = 4096
MODW = 2048
ACCS = 4
GBANKS = 3
NEG = -1.0e30
LEVELS = (1, 2, 4, 8, 16, 32, 64)
LAM_INIT = [0.8 - 0.6 * math.exp(-0.3 * l) for l in range(2)]


def column_map():
    at, n = {}, 0

    def put(name, width):
        nonlocal n
        at[name] = (n, width)
        n += width

    put("c1", 8)
    put("c2", 8)
    for l in range(2):
        for name, width in (("mix_g", 8), ("ffn_g", 8), ("lb", 4), ("hg_g", 1), ("qn_g", 1), ("kn_g", 1), ("lam", 4),
                            ("sub_g", 1), ("mod_b", 48)):
            put(f"a{l}_{name}", width)
    put("router", 64)
    for l in range(2):
        for name, width in (("mix_g", 8), ("ffn_g", 8), ("mod_b", 48), ("ql_g", 3), ("kl_g", 2), ("qn_g", 1),
                            ("qr_g", 1), ("kn_g", 1), ("kr_g", 1), ("bq_g", 1), ("bk_g", 1), ("dw_w", 4 * CONV_W),
                            ("dw_b", 4), ("ln_g", 4), ("ln_b", 4), ("pw_b", 8), ("fw", 132), ("fb", 44)):
            put(f"b{l}_{name}", width)
    return at, n


def constant_map():
    at, n = {}, 0

    def put(name, width):
        nonlocal n
        at[name] = (n, width)
        n += width

    for name, width in (("ident", 128), ("ones", 256), ("blk64", 128), ("blk32", 128), ("rot64", 128),
                        ("rot32", 128), ("mask", 256), ("levels", 128 * len(LEVELS)), ("alibi", 4 * 256),
                        ("before", 64), ("freq64", 1), ("freq32", 1)):
        put(name, width)
    return at, n


def constants():
    at, n = constant_map()
    c = np.zeros((P, n), np.float32)
    p, f = np.arange(P)[:, None], np.arange(P)[None, :]

    def put(name, value):
        o, w = at[name]
        c[:, o:o + w] = value

    put("ident", p == f)
    put("ones", 1.0)
    put("blk64", p // 64 == f // 64)
    put("blk32", p // 32 == f // 32)
    for w in (64, 32):
        h = w // 2
        same = p // w == f // w
        put(f"rot{w}", np.where(same & (p == f + h), -1.0, 0.0) + np.where(same & (p == f - h), 1.0, 0.0))
    dist = (P + p - np.arange(T)[None, :]).astype(np.float32)
    put("mask", np.where(dist < 0, NEG, 0.0))
    put("levels", np.concatenate([(p // (2 * s) == f // (2 * s)) & (p % (2 * s) < s) & (f % (2 * s) >= s)
                                  for s in LEVELS], 1))
    put("alibi", np.concatenate([np.where(dist < 0, NEG, -np.float32(2.0 ** (-8.0 * (h + 1) / 4)) * dist)
                                 for h in range(4)], 1))
    e, j = np.arange(8)[:, None], np.arange(8)[None, :]
    put("before", (j < e).astype(np.float32).reshape(1, 64))
    for name, w in (("freq64", 64), ("freq32", 32)):
        inv = (1.0 / (np.float32(10000.0) ** (np.arange(0, w, 2, dtype=np.float32) / np.float32(w)))).astype(np.float32)
        put(name, inv[np.arange(P) % (w // 2)][:, None])
    return c


def make_plan():
    plan, state = [], {"chunk": 0, "bank": 0, "side": 0, "ada": 0, "fence": 0}

    def chunk(name, idx, width, loop=False):
        c = dict(id=(name,) + tuple(idx), n=state["chunk"], slot=state["chunk"] % RING, name=name, idx=idx,
                 width=width, loop=loop)
        state["chunk"] += 1
        return c

    def unit(parts, rhs, evac, load, free, mode="F", tile=0, ready=(), after=()):
        u = dict(kind="unit", g=state["bank"], bank=state["bank"] % GBANKS, parts=parts, rhs=rhs, evac=evac,
                 load=load, free=free, mode=mode, tile=tile, ready=ready, after=after)
        state["bank"] += 1
        return u

    def side(kind, **kw):
        s = {"kind": kind, "s": state["side"], "needs": [], **kw}
        state["side"] += 1
        return s

    def fence():
        state["fence"] += 1
        return dict(kind="fence", n=state["fence"])

    def adas(layer, lo, hi):
        out = []
        for a in range(lo, hi):
            out.append(dict(kind="ada", n=state["ada"], layer=layer, a=a))
            state["ada"] += 1
        return out

    def f_units(name, idx, kt, cols, rhs, evacs, ready=()):
        c = chunk(name, idx, kt * cols)
        n = len(evacs)
        return [unit([(c, kt, cols, 256 * j, 0)], rhs, evacs[j], [c] if j == 0 else [], [c] if j == n - 1 else [],
                     ready=ready) for j in range(n)]

    def t_units(c, kt, cols, col, rhs, evacs, load, ready=()):
        return [unit([(c, kt, cols, col, 0)], rhs, evacs[t], load if t == 0 else [], [c] if t == 1 else [], mode="T",
                     tile=t, ready=ready) for t in range(2)]

    def merge(units, sides, lead=0, every=1):
        out, i = [], 0
        for n, u in enumerate(units):
            out.append(u)
            if n >= lead and (n - lead) % every == 0 and i < len(sides):
                out.append(sides[i])
                i += 1
        return out + sides[i:]

    def spread(items, extra, every):
        out, i, n = [], 0, 0
        for it in items:
            out.append(it)
            n += it["kind"] == "unit"
            if it["kind"] == "unit" and n % every == 0 and i < len(extra):
                out.append(extra[i])
                i += 1
        return out + extra[i:]

    def norm(src, nt, gain, dst, inv, total=False, mat="ones", const=1.0, post=None, needs=()):
        return side("norm", src=src, nt=nt, gain=gain, dst=dst, inv=inv, total=total, mat=mat, const=const,
                    post=post, needs=list(needs))

    def modulate(layer, pre, gname, shift, scale):
        return side("modcols", gain=f"{pre}_{gname}", shift=shift, scale=scale, layer=layer), \
            norm("x", 8, "A", "h", 1.0 / D, total=True, post=("shift", layer, shift))

    def attention(kind, v):
        steps = [(i, q) for i in range(4) for q in range(2)]
        return [side("attn", what=kind, v=v, load=steps[n] if n < 8 else None,
                     turn=steps[n - 1] if 0 <= n - 1 < 8 else None, out=steps[n - 2] if n >= 2 else None, needs=[])
                for n in range(10)]

    def with_needs(items, keys):
        items[0].setdefault("needs", [])
        items[0]["needs"] = list(items[0]["needs"]) + list(keys)
        return items

    def evac(kind, *args):
        return (kind,) + args

    def glu_units(name, pre, nu, evacs, loop=False):
        out = []
        for i in range(nu):
            c = chunk(name, pre + (i,), SLOT, loop)
            ea, eb = evacs(i)
            out.append(unit([(c, DK, 512, 0, 0)], "h", ea, [c], []))
            out.append(unit([(c, DK, 512, 256, 0)], "h", eb, [], [c]))
        return out

    def down_units(name, pre, kt, rhs, evacs, loop=False):
        out, half, ready = [], kt // 2, [("evac", state["bank"] - 1)]
        for i in range(4):
            cs = [chunk(name, pre + (i, k), half * 256, loop) for k in range(2)]
            out.append(unit([(cs[0], half, 256, 0, 0), (cs[1], half, 256, 0, half)], rhs, evacs(i), cs, cs,
                            ready=ready))
        return out

    plan.append(side("start", needs=[]))
    plan.extend(adas(0, 0, 8))
    for l in range(2):
        pre = f"a{l}"
        if l == 0:
            rest = adas(0, 8, 24)
        else:
            rest = adas(2, 0, 24)
        plan.extend(modulate(l, pre, "mix_g", 0, 8))
        plan.append(fence())
        w = "w_in1"
        q = f_units(w, (l, 0), DK, 512, "h", [evac("act", "Copy", "q", u) for u in range(2)])
        z = f_units(w, (l, 1), DK, 512, "h", [evac("act", "Copy", "z", u) for u in range(2)])
        cv = chunk(w, (l, 2), SLOT)
        v = t_units(cv, DK, 512, 0, "h", [evac("act", "Copy", "v", u) for u in range(2)], [cv])
        hg = f_units(w, (l, 3), DK, 512, "h", [evac("act", "Silu", "hg", u) for u in range(2)])
        dq = f_units(w, (l, 4), DK, 512, "h", [evac("act", "Copy", "dq", u) for u in range(2)])
        dk = f_units(w, (l, 5), DK, 512, "h", [evac("act", "Copy", "dk", u) for u in range(2)])
        cd = chunk(w, (l, 6), SLOT)
        dv = t_units(cd, DK, 512, 0, "h", [evac("act", "Copy", "dv", u) for u in range(2)], [cd])
        gates = []
        for i in range(4):
            gates += f_units(w, (l, 7 + i), DK, 512, "h",
                             [evac("act", "Sigmoid", "ga" if i < 2 else "gb", 2 * (i % 2) + u) for u in range(2)])
        sides = [side("hg_prep", layer=l, needs=[("evac", z[1]["g"])])]
        sides += [side("hg_level", level=n, needs=[]) for n in (0,) + LEVELS + (128,)]
        sides += [side("hg_out", needs=[("evac", v[1]["g"])])]
        sides += [norm("z", 4, f"{pre}_hg_g", "z", 1.0 / 128, post=("mul", "hg"), needs=[("evac", hg[1]["g"])])]
        sides += [norm("dq", 4, f"{pre}_qn_g", "dq", 1.0 / 64, mat="blk64", needs=[("evac", dk[1]["g"])])]
        sides += [norm("dk", 4, f"{pre}_kn_g", "dk", 1.0 / 64, mat="blk64"), side("lam", layer=l, needs=[])]
        sides += with_needs(attention("diff", "dv"), [("evac", dv[1]["g"])])
        sides += [norm("dq", 4, f"{pre}_sub_g", "dq", 1.0 / 128, const=1.0 - LAM_INIT[l])]
        items = merge(q + z + v + hg + dq + dk + dv + gates, sides, lead=4)
        plan.extend(spread(items, rest, 1))
        plan.append(fence())
        items = f_units("w_pa", (l,), 4, 1024, "z", [evac("gate", "ga", u, 0) for u in range(4)])
        items += f_units("w_pb", (l,), 4, 1024, "dq", [evac("gate", "gb", u, 1) for u in range(4)])
        plan.extend(items)
        plan.append(fence())
        for i in range(2):
            plan.extend(f_units("w_o1", (l, i), DK, 512, "h", [evac("resid", l, 16, 2 * i + u) for u in range(2)]))
        plan.append(fence())
        plan.extend(modulate(l, pre, "ffn_g", 24, 32))
        if l == 0:
            plan.append(fence())
            items = glu_units("f13", (), FF_U, lambda i: (evac("glu_a", i), evac("glu_b", i)))
            plan.extend(spread(items, adas(1, 0, 24), 1))
            plan.append(fence())
            plan.extend(down_units("f2", (), 22, "hid", lambda i: evac("resid", l, 40, i)))
            plan.append(fence())
        else:
            plan.append(side("router", needs=[]))
            plan.append(fence())
            while state["chunk"] % RING:
                state["chunk"] += 1
            while state["bank"] % GBANKS:
                state["bank"] += 1
            c0, g0 = state["chunk"], state["bank"]
            plan.append(dict(kind="loop", name="experts", count=EXPERTS))
            plan.extend(glu_units("m13", (), FE_U, lambda i: (evac("glu_a", i), evac("glu_b", i)), loop=True))
            plan.extend(down_units("m2", (), 28, "hid", lambda i: evac("expert", l, 40, i), loop=True))
            while state["chunk"] % RING:
                state["chunk"] += 1
            while state["bank"] % GBANKS:
                state["bank"] += 1
            plan.append(dict(kind="endloop", chunks=(c0, state["chunk"]), banks=(g0, state["bank"])))
            plan.append(fence())

    for l in range(2):
        pre, L = f"b{l}", 2 + l
        plan.extend(modulate(L, pre, "mix_g", 0, 8))
        if l == 0:
            plan.append(side("rope_tables", needs=[]))
        plan.append(fence())
        w = "w_in2"
        lat = f_units(w, (l, 0), DK, 512, "h", [evac("act", "Copy", "lat", u) for u in range(2)])
        lat += f_units("w_in2x", (l,), DK, 256, "h", [evac("act", "Copy", "lat", 2)])
        mq = f_units(w, (l, 1), DK, 512, "h", [evac("act", "Copy", "mq", u) for u in range(2)])
        mk = f_units(w, (l, 2), DK, 512, "h", [evac("act", "Copy", "mk", u) for u in range(2)])
        cv = chunk(w, (l, 3), SLOT)
        mv = t_units(cv, DK, 512, 0, "h", [evac("act", "Copy", "mv", u) for u in range(2)], [cv])
        ca = f_units(w, (l, 4), DK, 512, "h", [evac("conv_in", "Copy", u) for u in range(2)])
        cg = f_units(w, (l, 5), DK, 512, "h", [evac("conv_in", "Sigmoid", u) for u in range(2)])
        gates = []
        for i in range(6):
            gates += f_units(w, (l, 6 + i), DK, 512, "h",
                             [evac("act", "Sigmoid", "gates", 2 * i + u) for u in range(2)])
        gates[-1]["after"] = [("conv_gate_used", cg[1]["g"])]
        lat_norms = [norm("ql", 3, f"{pre}_ql_g", "ql", 1.0 / 384, total=True, needs=[("evac", lat[2]["g"])]),
                     norm("kl", 2, f"{pre}_kl_g", "kl", 1.0 / 256, total=True)]
        ready = [("side_done", s["s"]) for s in lat_norms]
        uq = f_units("w_uq", (l,), 3, 768, "ql",
                     [evac("act", "Copy", "qn", 0), evac("act", "Copy", "qn", 1), evac("act", "Copy", "qp", 0)],
                     ready=ready)
        ck = chunk("w_ukv", (l,), 2 * 1024)
        kn = [unit([(ck, 2, 1024, 256 * j, 0)], "kl", evac("act", "Copy", "kn", j), [ck] if j == 0 else [], [],
                   ready=ready) for j in range(2)]
        va = t_units(ck, 2, 1024, 512, "kl", [evac("act", "Copy", "va", u) for u in range(2)], [], ready=ready)
        sides = lat_norms
        sides += [norm("kr", 1, f"{pre}_kr_g", "kr", 1.0 / 32, mat="blk32", post=("rope", "32"))]
        sides += [norm("mq", 4, f"{pre}_bq_g", "mq", 1.0 / 64, mat="blk64", post=("rope", "64"),
                       needs=[("evac", mk[1]["g"])]),
                  norm("mk", 4, f"{pre}_bk_g", "mk", 1.0 / 64, mat="blk64", post=("rope", "64"))]
        moba = with_needs(attention("moba", "mv"), [("evac", mv[1]["g"])])
        conv = lambda t: [side("conv", tile=t, layer=l, needs=[("evac", cg[1]["g"]), ("unit", va[1]["g"])])]
        sides += moba
        sides += [norm("qn", 4, f"{pre}_qn_g", "qn", 1.0 / 64, mat="blk64", needs=[("evac", va[1]["g"])])]
        sides += [norm("kn", 4, f"{pre}_kn_g", "kn", 1.0 / 64, mat="blk64")]
        sides += [norm("qp", 2, f"{pre}_qr_g", "qp", 1.0 / 32, mat="blk32", post=("rope", "32"))]
        sides += attention("mla", "va")
        for t in range(4):
            sides += conv(t)
        sides += [side("center", needs=[])]
        sides += [norm("ca", 4, f"{pre}_ln_g", "ca", 1.0 / 512, total=True, post=("silu", f"{pre}_ln_b"))]
        units = lat + mq + mk + mv + uq + kn + va + ca + cg + gates
        items = units[:3] + [sides[0], sides[1]] + merge(units[3:], sides[2:], lead=4)
        if l == 0:
            items = spread(items, adas(2, 24, 24), 1)
        plan.extend(items)
        plan.append(fence())
        items = f_units("w_mla", (l,), 4, 1024, "qn", [evac("gate", "g0", u, 0) for u in range(4)])
        items += f_units("w_moba", (l,), 4, 1024, "mq", [evac("gate", "g1", u, 1) for u in range(4)])
        items += f_units("w_pw", (l,), 4, 1024, "ca", [evac("gate_bias", "g2", u, f"{pre}_pw_b") for u in range(4)])
        plan.extend(items)
        plan.append(fence())
        for i in range(2):
            plan.extend(f_units("w_o2", (l, i), DK, 512, "h", [evac("resid", L, 16, 2 * i + u) for u in range(2)]))
        plan.append(fence())
        plan.extend(modulate(L, pre, "ffn_g", 24, 32))
        plan.append(fence())
        items = glu_units("up", (l,), FF_U, lambda i: (evac("fir_a", l, i), evac("fir_b", l, i)))
        if l == 0:
            items = spread(items, adas(3, 0, 24), 1)
        plan.extend(items)
        plan.append(fence())
        plan.extend(down_units("down", (l,), 22, "hid", lambda i: evac("resid", L, 40, i)))
        plan.append(fence())
    plan.append(dict(kind="end"))
    return plan


class Book:

    def __init__(self):
        self.known, self.grown = {}, {}
        self.restart()

    def restart(self):
        self.at, self.count = {}, {}


class Count:

    def __init__(self, name, book):
        self.name, self.book, self.round, self.entry = name, book, None, None

    def step(self, *keys, of=None, by=1):
        name = of or self.name
        self.book.count[name] = self.book.count.get(name, 0) + by
        for key in keys:
            self.mark(*key, of=name)
        return by

    def mark(self, *key, of=None):
        name = of or self.name
        self.book.at[key] = (name, self.book.count.get(name, 0), self.round is not None)

    def value(self, name, count, looped, last_round=False):
        grown = self.book.grown.get(name, 0) if looped else 0
        if looped and self.round is not None and grown:
            count -= grown if last_round else 0
            assert count > 0, name
            return self.round * grown + count
        return count + (EXPERTS - 1) * grown

    def at(self, *key, last_round=False):
        return self.value(*self.book.known[key], last_round) if key in self.book.known else 0

    def by(self, *key):
        return self.book.known.get(key, (self.name,))[0]

    def now(self):
        return self.value(self.name, self.book.count.get(self.name, 0), self.round is not None)

    def begin_rounds(self, register):
        self.round, self.entry = register, dict(self.book.count)

    def end_rounds(self):
        for name, count in self.book.count.items():
            if count > self.entry.get(name, 0):
                self.book.grown[name] = count - self.entry.get(name, 0)
                self.book.count[name] += (EXPERTS - 1) * self.book.grown[name]
        self.round = None


def build(nc, arrays, out, book, ccols, ccons):
    colat, ncol = column_map()
    conat, ncon = constant_map()
    plan = make_plan()
    with ExitStack() as ctx:
        def sb(name, shape, dt=F32):
            return ctx.enter_context(nc.sbuf_tensor(name, shape, dt))

        xT = sb("xT", [P, 8, T])
        hT = sb("hT", [P, 8, T])
        ring = sb("ring", [P, RING, SLOT])
        mod_in = sb("mod_in", [P, 2, MODW])
        mod_acc = sb("mod_acc", [P, ACCS, 256])
        ada = sb("ada", [P, 2, 48])
        act_c = sb("act_c", [P, 2, 8])
        acol = sb("acol", [P, 8])
        cols = sb("cols", [P, ncol])
        cons = sb("cons", [P, ncon])
        small = sb("small", [P, 160])
        WN = 22144
        pos = sb("pos", [P, T], I32)
        work = sb("work", [P, WN])
        psum = ctx.enter_context(nc.psum_tensor("psum", [P, 8, 512], F32))

        def region(off, nt, w=T):
            return work[:, off:off + nt * w].rearrange("p (a b) -> p a b", b=w)

        R = {"x": xT[:, :, :], "h": hT[:, :, :]}
        off = 0
        for name, nt in (("q", 4), ("z", 4), ("hg", 4), ("dq", 4), ("dk", 4), ("ga", 8), ("gb", 8)):
            R[name] = region(off, nt)
            off += nt * T
        for name in ("v", "dv"):
            R[name] = region(off, 2, 512)
            off += 1024
        hb = off
        for name in ("b", "e", "qt", "kt", "kin"):
            R[name] = region(off, 4)
            off += 1024
        R["sc"] = region(off, 3, 512)
        off += 1536
        assert off <= WN
        off = 0
        R["lat"] = region(off, 6)
        R["ql"], R["kl"], R["kr"] = region(off, 3), region(off + 3 * T, 2), region(off + 5 * T, 1)
        R["ca"] = region(off, 4)
        off += 6 * T
        for name, nt in (("mq", 4), ("mk", 4), ("gates", 24), ("qn", 4), ("kn", 4), ("qp", 2)):
            R[name] = region(off, nt)
            off += nt * T
        R["g0"], R["g1"], R["g2"] = R["gates"][:, 0:8, :], R["gates"][:, 8:16, :], R["gates"][:, 16:24, :]
        for name in ("mv", "va"):
            R[name] = region(off, 2, 512)
            off += 1024
        PADT = T + CONV_W - 1
        R["cu"] = region(off, 4, PADT)
        off += 4 * PADT
        R["cos64"], R["sin64"], R["cos32"], R["sin32"] = (region(off + i * T, 1) for i in range(4))
        off += 4 * T
        temp2 = off
        assert temp2 + 4096 + 1536 <= WN, temp2
        R["hid"] = region(0, 28)
        R["comb"] = region(28 * T, 8)
        R["silu"] = region(36 * T, 4)
        R["weighted"] = region(40 * T, 2)
        comb_off = 28 * T
        R["fir"] = region(44 * T, 8)
        assert 52 * T <= temp2 - 1024
        R["conv_gate"] = R["gates"][:, 22:24, :]

        def temps(s_item):
            base = temp2 if s_item.get("block2") else hb
            sq = region(base, 8)
            return sq, region(base + 2048, 4), region(base + 3072, 4), region(base, 4)

        def soft(s_item):
            base = (temp2 + 4096) if s_item.get("block2") else hb + 4096
            return (work[:, base:base + 512].rearrange("p (c n) -> p c n", c=2),
                    work[:, base + 512:base + 1024].rearrange("p (c n) -> p c n", c=2),
                    work[:, base + 1024:base + 1536])

        block2 = False
        for it in plan:
            if it["kind"] == "rope_tables":
                block2 = True
            it["block2"] = block2

        def col(name, i=0, n=1):
            o, w = colat[name]
            assert i + n <= w
            return cols[:, o + i:o + i + n]

        def con(name, i=0, n=None):
            o, w = conat[name]
            return cons[:, o + i:o + (i + n if n else w)]

        def gbank(b):
            return psum[:, b, :].rearrange("p (a t) -> p a t", t=T)

        def sbank(i):
            return psum[:, GBANKS + i, :]

        ada_bank = psum[:, 7, :]
        in_loop = [u for u in plan if u["kind"] == "unit" and u["parts"][0][0]["loop"]]
        last_glu = [max([u["g"] for u in in_loop if u["evac"][0] == "glu_b" and u["evac"][1] % 2 == i], default=0)
                    for i in range(2)]
        last_down = max([u["g"] for u in in_loop], default=0)

        def sem(name):
            return ctx.enter_context(nc.semaphore(name))

        tensor_done, scalar_done = sem("tensor_done"), sem("scalar_done")
        vector_done, gpsimd_done = sem("vector_done"), sem("gpsimd_done")
        inputs_loaded, stored = sem("inputs_loaded"), sem("stored")
        slot_loaded = [sem(f"slot{i}_loaded") for i in range(RING)]
        mod_loaded = [sem(f"mod{i}_loaded") for i in range(2)]
        done = {"PE": tensor_done, "ACT": scalar_done, "DVE": vector_done, "POOL": gpsimd_done}
        book.restart()
        cut = [i for i, it in enumerate(plan) if it["kind"] in ("loop", "endloop")]
        before, experts, after = (plan[:cut[0]], plan[cut[0] + 1:cut[1]], plan[cut[1] + 1:]) if cut else (plan, [], [])

        block = ctx.enter_context(nc.Block())

        @block.sync
        def _(sp):
            w = Count("SP", book)
            used, fences = {}, []
            sp.dma_start(cols[:, :], ccols).then_inc(inputs_loaded, w.step(of="inputs", by=16))
            sp.dma_start(cons[:, :], ccons).then_inc(inputs_loaded, w.step(of="inputs", by=16))
            sp.dma_start(xT[:, :, :], arrays["xT"]).then_inc(inputs_loaded, w.step(of="inputs", by=16))
            sp.dma_start(pos[:, :], arrays["positions"].to_broadcast([P, T])).then_inc(
                inputs_loaded, w.step(("inputs",), of="inputs", by=16))

            def run(steps):
                for it in steps:
                    if it["kind"] == "fence":
                        fences.append(it["n"])
                    for c in it["load"] if it["kind"] == "unit" else ():
                        last = used.get(c["slot"])
                        if c["loop"] and (last is None or not last["loop"]):
                            n = [d["n"] for u in experts for d in u["load"] if d["slot"] == c["slot"]][-1]
                            sp.wait_ge(tensor_done, w.at("used", n, last_round=True))
                        elif last is not None:
                            sp.wait_ge(tensor_done, w.at("used", last["n"]))
                        used[c["slot"]] = c
                        src = arrays[c["name"]]
                        for i in ((w.round,) if c["loop"] else ()) + tuple(c["idx"]):
                            src = src[i]
                        sp.dma_start(ring[:, c["slot"], 0:c["width"]], src).then_inc(
                            slot_loaded[c["slot"]], w.step(("loaded", c["n"]), of=f"slot{c['slot']}", by=16))

            run(before)
            if experts:
                for c in used.values():
                    sp.wait_ge(tensor_done, w.at("used", c["n"]))
                with sp.Fori(0, EXPERTS) as e:
                    w.begin_rounds(e)
                    run(experts)
                    w.end_rounds()
            run(after)
            sp.wait_ge(vector_done, w.at("fence", fences[-1], "DVE"))
            sp.dma_start(out, xT[:, :, :]).then_inc(stored, 16)
            sp.wait_ge(stored, 16)

        @block.tensor
        def _(pe):
            w = Count("PE", book)

            def begin(it):
                if it["s"]:
                    pe.wait_ge(tensor_done, w.at("side", it["s"] - 1, "PE"))
                    pe.wait_ge(scalar_done, w.at("side", it["s"] - 1, "ACT"))
                    pe.wait_ge(vector_done, w.at("side", it["s"] - 1, "DVE"))
                for key in it["needs"]:
                    pe.wait_ge(done[w.by(*key)], w.at(*key))

            def fence(it):
                w.mark("fence", it["n"], "PE")
                pe.wait_ge(scalar_done, w.at("fence", it["n"], "ACT"))
                pe.wait_ge(vector_done, w.at("fence", it["n"], "DVE"))

            mm, ev = nc.tensor.matmul, {}
            loop_gs = [u["g"] for u in in_loop]

            def unit(it):
                g = it["g"]
                looped = it["parts"][0][0]["loop"]
                prev = ev.get(it["bank"])
                if looped and (prev is None or prev not in loop_gs):
                    last = ("evac", max(x for x in loop_gs if x % GBANKS == it["bank"]))
                    pe.wait_ge(done[w.by(*last)], w.at(*last, last_round=True))
                elif prev is not None:
                    pe.wait_ge(done[w.by("evac", prev)], w.at("evac", prev))
                ev[it["bank"]] = g
                for key in it["ready"]:
                    if key[0] == "side_done":
                        pe.wait_ge(vector_done, w.at("side", key[1], "DVE"))
                    else:
                        pe.wait_ge(done[w.by(*key)], w.at(*key))
                rhs = R[it["rhs"]]
                total = sum(p[1] for p in it["parts"])
                n = 0
                if it["mode"] == "F":
                    for j in range(2):
                        n = 0
                        for c, kt, width, col0, k0 in it["parts"]:
                            pe.wait_ge(slot_loaded[c["slot"]], w.at("loaded", c["n"]))
                            wt = ring[:, c["slot"], 0:kt * width].rearrange("p (k n) -> p k n", n=width)
                            for k in range(kt):
                                last = mm(gbank(it["bank"])[:, j, :], wt[:, k, col0 + j * P:col0 + (j + 1) * P],
                                          rhs[:, k0 + k, :], start=(n == 0), stop=(n == total - 1))
                                n += 1
                else:
                    (c, kt, width, col0, k0), = it["parts"]
                    pe.wait_ge(slot_loaded[c["slot"]], w.at("loaded", c["n"]))
                    wt = ring[:, c["slot"], 0:kt * width].rearrange("p (k n) -> p k n", n=width)
                    for k in range(kt):
                        last = mm(psum[:, it["bank"], :], rhs[:, k, it["tile"] * P:(it["tile"] + 1) * P],
                                  wt[:, k, col0:col0 + 512], start=(k == 0), stop=(k == kt - 1))
                last.then_inc(tensor_done, w.step(("unit", g), *[("used", c["n"]) for c in it["free"]]))

            def ada_step(it):
                n = it["n"]
                pe.wait_ge(gpsimd_done, w.at("mod_acc", n))
                if n:
                    pe.wait_ge(vector_done, w.at("ada", n - 1))
                for j in range(2):
                    last = mm(ada_bank[:, j:j + 1], mod_acc[:, n % ACCS, j * P:(j + 1) * P], con("ones", 0, 1),
                              start=True, stop=True)
                last.then_inc(tensor_done, w.step(("ada_sum", n)))

            def norm(it):
                begin(it)
                sq = temps(it)[0]
                pe.wait_ge(scalar_done, w.at("squares", it["s"]))
                nt = it["nt"]
                for t in range(nt):
                    if it["total"]:
                        last = mm(sbank(0)[:, 0:T], con(it["mat"], 0, P), sq[:, t, :], start=(t == 0), stop=(t == nt - 1))
                    else:
                        last = mm(sbank(t // 2)[:, (t % 2) * T:(t % 2 + 1) * T], con(it["mat"], 0, P), sq[:, t, :],
                                  start=True, stop=True)
                last.then_inc(tensor_done, w.step(("sums", it["s"])))
                if it["post"] and it["post"][0] == "rope":
                    pe.wait_ge(vector_done, w.at("scaled", it["s"]))
                    for t in range(nt):
                        last = mm(sbank(2 + t // 2)[:, (t % 2) * T:(t % 2 + 1) * T], con("rot" + it["post"][1]),
                                  R[it["dst"]][:, t, :], start=True, stop=True)
                    last.then_inc(tensor_done, w.step(("turned", it["s"])))

            def hg_level(it):
                begin(it)
                n = it["level"]
                k, q = (R["kin"], R["q"]) if n == 0 else (R["kt"], R["qt"])
                pe.wait_ge(vector_done, w.at("decayed", it["s"]))
                if n == 128:
                    for h in range(4):
                        last = mm(sbank(0)[:, h * P:(h + 1) * P], k[:, h, 0:P], q[:, h, P:T], start=True, stop=True)
                else:
                    for t in range(2):
                        for h in range(4):
                            last = mm(sbank(t)[:, h * P:(h + 1) * P], k[:, h, t * P:(t + 1) * P],
                                      q[:, h, t * P:(t + 1) * P], start=True, stop=True)
                last.then_inc(tensor_done, w.step(("level", it["s"])))

            def hg_out(it):
                begin(it)
                v, sc = R["v"], R["sc"]
                for h in range(4):
                    o = sbank(2 + h // 2)[:, (h % 2) * T:(h % 2 + 1) * T]
                    cut = slice(h * P, (h + 1) * P)
                    mm(o[:, 0:P], v[:, 0, cut], sc[:, 0, cut], start=True, stop=True)
                    mm(o[:, P:T], v[:, 0, cut], sc[:, 1, cut], start=True, stop=False)
                    last = mm(o[:, P:T], v[:, 1, cut], sc[:, 2, cut], start=False, stop=True)
                last.then_inc(tensor_done, w.step(("hg_o", it["s"])))

            def attn(it):
                begin(it)
                soft_s, soft_w, turned = soft(it)
                what = it["what"]
                if it["out"]:
                    i, q = it["out"]
                    v = R[it["v"]]
                    for c in range(1 if what == "diff" else 2):
                        for kt in range(q + 1):
                            last = mm(sbank(3)[:, c * P:(c + 1) * P], v[:, kt, i * P:(i + 1) * P],
                                      turned[:, (c * 2 + kt) * P:(c * 2 + kt + 1) * P], start=(kt == 0), stop=(kt == q))
                    last.then_inc(tensor_done, w.step(("attn_out", it["s"])))
                if it["turn"]:
                    i, q = it["turn"]
                    for c in range(1 if what == "diff" else 2):
                        for kt in range(q + 1):
                            last = nc.tensor.transpose(sbank(2)[:, (c * 2 + kt) * P:(c * 2 + kt + 1) * P],
                                                       soft_w[:, c, kt * P:(kt + 1) * P], con("ident"))
                    last.then_inc(tensor_done, w.step(("attn_turn", it["s"])))
                if it["load"]:
                    i, q = it["load"]
                    n = (q + 1) * P
                    for c in range(2):
                        o = sbank(c)[:, 0:n]
                        rows = slice(c * 64, c * 64 + 64)
                        Q, K = {"diff": ("dq", "dk"), "moba": ("mq", "mk"), "mla": ("qn", "kn")}[what]
                        last = mm(o, R[Q][rows, i, q * P:(q + 1) * P], R[K][rows, i, 0:n], start=True,
                                  stop=(what != "mla"))
                        if what == "mla":
                            last.then_inc(tensor_done, w.step())
                            pe.wait_ge(tensor_done, w.now())
                            h = 2 * i + c
                            rows = slice((h % 4) * 32, (h % 4) * 32 + 32)
                            last = mm(o, R["qp"][rows, h // 4, q * P:(q + 1) * P], R["kr"][rows, 0, 0:n],
                                      start=False, stop=True)
                    last.then_inc(tensor_done, w.step(("scores", it["s"])))

            def run(steps):
                for it in steps:
                    kind = it["kind"]
                    if kind == "unit":
                        unit(it)
                    elif kind == "ada":
                        ada_step(it)
                    elif kind == "fence":
                        fence(it)
                    elif kind == "end":
                        pass
                    else:
                        if kind == "norm":
                            norm(it)
                        elif kind == "hg_level":
                            hg_level(it)
                        elif kind == "hg_out":
                            hg_out(it)
                        elif kind == "attn":
                            attn(it)
                        elif kind == "lam":
                            begin(it)
                            pe.wait_ge(vector_done, w.at("lam_products", it["s"]))
                            mm(sbank(0)[:, 0:2], con("blk64"), small[:, 0:2], start=True, stop=True).then_inc(tensor_done, w.step(("lam_sums", it["s"])))
                        elif kind == "center":
                            begin(it)
                            for t in range(4):
                                last = mm(sbank(0)[:, 0:T], con("ones", 0, P), R["ca"][:, t, :], start=(t == 0), stop=(t == 3))
                            last.then_inc(tensor_done, w.step(("center", it["s"])))
                        elif kind == "router":
                            begin(it)
                            for t in range(2):
                                for k in range(DK):
                                    last = mm(sbank(0)[:, t * 8:t * 8 + 8], R["h"][:, k, t * P:(t + 1) * P],
                                              col("router", 8 * k, 8), start=(k == 0), stop=(k == DK - 1))
                            last.then_inc(tensor_done, w.step(("logits", it["s"])))
                            pe.wait_ge(vector_done, w.at("diagonals", it["s"]))
                            dg = region(hb, 8)
                            for e in range(EXPERTS):
                                for t in range(2):
                                    last = mm(sbank(e // 2)[:, (e % 2) * T + t * P:(e % 2) * T + (t + 1) * P],
                                              con("ones", 0, P), dg[:, e, t * P:(t + 1) * P], start=True, stop=True)
                            last.then_inc(tensor_done, w.step(("comb", it["s"])))
                        w.mark("side", it["s"], w.name)

            run(before)
            if experts:
                with pe.Fori(0, EXPERTS) as e:
                    w.begin_rounds(e)
                    run(experts)
                    w.end_rounds()
            run(after)

        @block.scalar
        def _(act):
            w = Count("ACT", book)

            def begin(it):
                if it["s"]:
                    act.wait_ge(scalar_done, w.at("side", it["s"] - 1, "ACT"))
                    act.wait_ge(tensor_done, w.at("side", it["s"] - 1, "PE"))
                    act.wait_ge(vector_done, w.at("side", it["s"] - 1, "DVE"))
                for key in it["needs"]:
                    act.wait_ge(done[w.by(*key)], w.at(*key))

            def fence(it):
                w.mark("fence", it["n"], "ACT")
                act.wait_ge(tensor_done, w.at("fence", it["n"], "PE"))
                act.wait_ge(vector_done, w.at("fence", it["n"], "DVE"))

            A = nc.scalar.activation

            def unit(it):
                e, g = it["evac"], it["g"]
                if e[0] == "act":
                    act.wait_ge(tensor_done, w.at("unit", g))
                    for key in it["after"]:
                        act.wait_ge(vector_done, w.at(*key))
                    if it["mode"] == "F":
                        dst, src = R[e[2]][:, 2 * e[3]:2 * e[3] + 2, :], gbank(it["bank"])
                    else:
                        dst, src = R[e[2]][:, e[3], :], psum[:, it["bank"], :]
                    A(dst, src, {"Copy": ACT.Copy, "Silu": ACT.Silu, "Sigmoid": ACT.Sigmoid}[e[1]]).then_inc(scalar_done, w.step(("evac", g)))
                elif e[0] == "conv_in":
                    act.wait_ge(tensor_done, w.at("unit", g))
                    u = e[2]
                    if e[1] == "Copy":
                        A(R["cu"][:, 2 * u:2 * u + 2, CONV_W - 1:PADT], gbank(it["bank"]), ACT.Copy).then_inc(scalar_done, w.step(("evac", g)))
                    else:
                        act.wait_ge(vector_done, w.at("conv_gate_used", it["g"] - 1))
                        A(R["conv_gate"], gbank(it["bank"]), ACT.Sigmoid).then_inc(scalar_done, w.step(("evac", g)))
                elif e[0] == "glu_a":
                    act.wait_ge(tensor_done, w.at("unit", g))
                    if it["parts"][0][0]["loop"] and e[1] < 2:
                        act.wait_ge(vector_done, w.at("evac", last_glu[e[1]], last_round=True))
                    else:
                        if e[1] >= 2:
                            act.wait_ge(vector_done, w.at("evac", g - 3))
                    A(R["silu"][:, 2 * (e[1] % 2):2 * (e[1] % 2) + 2, :], gbank(it["bank"]), ACT.Silu).then_inc(scalar_done, w.step(("glu_a", g)))
                    w.mark("evac", g)
                elif e[0] in ("fir_a", "fir_b"):
                    act.wait_ge(tensor_done, w.at("unit", g))
                    l, i = e[1], e[2]
                    act.wait_ge(vector_done, w.at("fir_used", g - 2))
                    b = 4 * (i % 2) + (2 if e[0] == "fir_b" else 0)
                    for j in range(2):
                        tile = (0 if e[0] == "fir_a" else 22) + 2 * i + j
                        A(R["fir"][:, b + j, :], gbank(it["bank"])[:, j, :], ACT.Identity,
                                 bias=col(f"b{l}_fb", tile), scale=col(f"b{l}_fw", 2 * 44 + tile)).then_inc(scalar_done, w.step(("fir_0", g)))
                    if e[0] == "fir_b":
                        a = 4 * (i % 2)
                        act.wait_ge(vector_done, w.at("fir_sum", g - 1))
                        act.wait_ge(scalar_done, w.now())
                        A(R["fir"][:, a:a + 2, :], R["fir"][:, a:a + 2, :], ACT.Silu).then_inc(scalar_done, w.step(("fir_silu", g)))

            def norm(it):
                begin(it)
                sq, t1, y, _ = temps(it)
                nt = it["nt"]
                src = R[it["src"]]
                n = T if it["total"] else nt * T
                A(sq[:, 0:nt, :], src[:, 0:nt, :], ACT.Square).then_inc(scalar_done, w.step(("squares", it["s"])))
                act.wait_ge(vector_done, w.at("mean", it["s"]))
                nn = 1 if it["total"] else nt
                A(y[:, 0:nn, :], t1[:, 0:nn, :], ACT.Ln).then_inc(scalar_done, w.step())
                act.wait_ge(scalar_done, w.now())
                A(y[:, 0:nn, :], y[:, 0:nn, :], ACT.Exp, scale=-0.5).then_inc(scalar_done, w.step(("root", it["s"])))
                post = it["post"]
                if post and post[0] == "shift":
                    for t in range(nt):
                        act.wait_ge(vector_done, w.at("scaled_tile", it["s"], t))
                        A(R["h"][:, t, :], R["h"][:, t, :], ACT.Identity,
                                 bias=ada[:, post[1] % 2, post[2] + t:post[2] + t + 1]).then_inc(scalar_done, w.step())
                if post and post[0] == "silu":
                    for t in range(nt):
                        act.wait_ge(vector_done, w.at("scaled_tile", it["s"], t))
                        A(R[it["dst"]][:, t, :], R[it["dst"]][:, t, :], ACT.Silu, bias=col(post[1], t)).then_inc(scalar_done, w.step())

            def hg_prep(it):
                begin(it)
                A(R["kin"], R["z"], ACT.Sigmoid, scale=-1.0).then_inc(scalar_done, w.step(("kin", it["s"])))
                if it["layer"] == 0:
                    act.wait_ge(vector_done, w.at("abs_z", it["s"]))
                    A(R["e"], R["e"], ACT.Exp, scale=-1.0).then_inc(scalar_done, w.step())
                    act.wait_ge(scalar_done, w.now())
                    A(R["e"], R["e"], ACT.Ln, bias=1.0).then_inc(scalar_done, w.step(("softplus", it["s"])))
                else:
                    A(R["e"], R["z"], ACT.Sigmoid).then_inc(scalar_done, w.step())
                    act.wait_ge(vector_done, w.at("lb_in", it["s"]))
                    A(small[:, 8:12], small[:, 8:12], ACT.Sigmoid).then_inc(scalar_done, w.step(("lb", it["s"])))
                    act.wait_ge(vector_done, w.at("forget", it["s"]))
                    A(R["qt"], R["e"], ACT.Ln).then_inc(scalar_done, w.step(("log_f", it["s"])))

            def attn(it):
                begin(it)
                soft_s, soft_w, turned = soft(it)
                what = it["what"]
                if it["turn"]:
                    i, q = it["turn"]
                    act.wait_ge(tensor_done, w.at("attn_turn", it["s"]))
                    act.wait_ge(tensor_done, w.at("attn_out", it["s"]))
                    for c in range(1 if what == "diff" else 2):
                        n = (q + 1) * P
                        last = A(turned[:, c * 256:c * 256 + n], sbank(2)[:, c * 256:c * 256 + n], ACT.Copy)
                        last.then_inc(scalar_done, w.step())
                if it["load"]:
                    i, q = it["load"]
                    n = (q + 1) * P
                    act.wait_ge(vector_done, w.at("neg_max", it["s"]))
                    for c in range(2):
                        A(soft_s[:, c, 0:n], soft_s[:, c, 0:n], ACT.Exp, bias=small[:, 22 + c:23 + c],
                                 accum_out=small[:, 24 + c:25 + c]).then_inc(scalar_done, w.step(("exps", it["s"])))

            def run(steps):
                for it in steps:
                    kind = it["kind"]
                    if kind == "unit":
                        unit(it)
                    elif kind == "fence":
                        fence(it)
                    elif kind in ("ada", "end"):
                        pass
                    else:
                        if kind == "norm":
                            norm(it)
                        elif kind == "start":
                            act.wait_ge(inputs_loaded, w.at("inputs"))
                            A(act_c[:, 0, :], col("c1", 0, 8), ACT.Silu).then_inc(scalar_done, w.step())
                            A(act_c[:, 1, :], col("c2", 0, 8), ACT.Silu).then_inc(scalar_done, w.step(("silu_c",)))
                        elif kind == "hg_prep":
                            hg_prep(it)
                        elif kind == "hg_level" and it["level"] > 0:
                            begin(it)
                            act.wait_ge(vector_done, w.at("spans", it["s"]))
                            A(R["e"], R["e"], ACT.Exp).then_inc(scalar_done, w.step(("decays", it["s"])))
                        elif kind == "hg_out":
                            begin(it)
                            act.wait_ge(tensor_done, w.at("hg_o", it["s"]))
                            for i in range(2):
                                A(R["z"][:, 2 * i:2 * i + 2, :], sbank(2 + i).rearrange("p (a t) -> p a t", t=T),
                                         ACT.Copy).then_inc(scalar_done, w.step())
                        elif kind == "attn":
                            attn(it)
                        elif kind == "lam":
                            begin(it)
                            act.wait_ge(tensor_done, w.at("lam_sums", it["s"]))
                            A(small[:, 2:4], sbank(0)[:, 0:2], ACT.Exp).then_inc(scalar_done, w.step(("lam_exps", it["s"])))
                        elif kind == "router":
                            begin(it)
                            act.wait_ge(vector_done, w.at("neg_max", it["s"]))
                            for t in range(2):
                                A(small[:, 64 + 8 * t:72 + 8 * t], small[:, 48 + 8 * t:56 + 8 * t], ACT.Exp,
                                         bias=small[:, 82 + t:83 + t]).then_inc(scalar_done, w.step(("exps", it["s"])))
                        elif kind == "rope_tables":
                            begin(it)
                            for j, name in enumerate(("64", "32")):
                                act.wait_ge(vector_done, w.at("angle", it["s"], j))
                                A(R["sin" + name], R["cos" + name], ACT.Sin).then_inc(scalar_done, w.step(("sin", it["s"], j)))
                                A(R["cos" + name], R["cos" + name], ACT.Sin, scale=0.5).then_inc(scalar_done, w.step(("half", it["s"], j)))
                        w.mark("side", it["s"], w.name)

            run(before)
            if experts:
                with act.Fori(0, EXPERTS) as e:
                    w.begin_rounds(e)
                    run(experts)
                    w.end_rounds()
            run(after)

        @block.vector
        def _(dve):
            w = Count("DVE", book)

            def begin(it):
                if it["s"]:
                    dve.wait_ge(vector_done, w.at("side", it["s"] - 1, "DVE"))
                    dve.wait_ge(tensor_done, w.at("side", it["s"] - 1, "PE"))
                    dve.wait_ge(scalar_done, w.at("side", it["s"] - 1, "ACT"))
                for key in it["needs"]:
                    dve.wait_ge(done[w.by(*key)], w.at(*key))

            def fence(it):
                w.mark("fence", it["n"], "DVE")
                dve.wait_ge(tensor_done, w.at("fence", it["n"], "PE"))
                dve.wait_ge(scalar_done, w.at("fence", it["n"], "ACT"))

            V = nc.vector

            def op(ins, *keys):
                ins.then_inc(vector_done, w.step(*keys))

            def unit(it):
                e, g = it["evac"], it["g"]
                kind = e[0]
                if kind in ("act", "glu_a"):
                    return
                if kind == "conv_in":
                    if e[1] == "Sigmoid":
                        u = e[2]
                        dve.wait_ge(scalar_done, w.at("evac", g))
                        cu = R["cu"][:, 2 * u:2 * u + 2, CONV_W - 1:PADT]
                        V.tensor_tensor(cu, cu, R["conv_gate"], ALU.mult).then_inc(vector_done, w.step(("conv_gate_used", g)))
                        w.mark("evac_all", g)
                    return
                if kind == "fir_a" or kind == "fir_b":
                    l, i = e[1], e[2]
                    b = 4 * (i % 2) + (2 if kind == "fir_b" else 0)
                    dve.wait_ge(scalar_done, w.at("fir_0", g))
                    for tap in (1, 0):
                        dve.wait_ge(vector_done, w.now())
                        d = 2 - tap
                        for j in range(2):
                            tile = (0 if kind == "fir_a" else 22) + 2 * i + j
                            o = R["fir"][:, b + j, d:T]
                            last = V.scalar_tensor_tensor(out=o, in0=gbank(it["bank"])[:, j, 0:T - d],
                                                          scalar=col(f"b{l}_fw", tap * 44 + tile), in1=o, op0=ALU.mult,
                                                          op1=ALU.add)
                            last.then_inc(vector_done, w.step())
                    w.mark("evac", g)
                    w.mark("fir_sum", g)
                    if kind == "fir_b":
                        dve.wait_ge(scalar_done, w.at("fir_silu", g))
                        dve.wait_ge(vector_done, w.now())
                        a = 4 * (i % 2)
                        V.tensor_tensor(R["hid"][:, 2 * i:2 * i + 2, :], R["fir"][:, a:a + 2, :],
                                           R["fir"][:, a + 2:a + 4, :], ALU.mult).then_inc(vector_done, w.step(("fir_used", g + 2), ("fir_used", g + 1)))
                    return
                dve.wait_ge(tensor_done, w.at("unit", g))
                ps = gbank(it["bank"])
                if kind == "glu_b":
                    i = e[1]
                    dve.wait_ge(scalar_done, w.at("glu_a", g - 1))
                    if it["parts"][0][0]["loop"] and i == 0:
                        dve.wait_ge(vector_done, w.now())
                        dve.wait_ge(tensor_done, w.at("unit", last_down, last_round=True))
                    V.tensor_tensor(R["hid"][:, 2 * i:2 * i + 2, :], ps, R["silu"][:, 2 * (i % 2):2 * (i % 2) + 2, :],
                                       ALU.mult).then_inc(vector_done, w.step(("evac", g)))
                elif kind == "gate":
                    _, name, u, add = e
                    y, gate = R["h"][:, 2 * u:2 * u + 2, :], R[name][:, 2 * u:2 * u + 2, :]
                    if not add:
                        V.tensor_tensor(y, ps, gate, ALU.mult).then_inc(vector_done, w.step(("evac", g)))
                    else:
                        V.tensor_tensor(gate, ps, gate, ALU.mult).then_inc(vector_done, w.step(("evac", g)))
                        dve.wait_ge(vector_done, w.now())
                        V.tensor_tensor(y, y, gate, ALU.add).then_inc(vector_done, w.step())
                elif kind == "gate_bias":
                    _, name, u, bias = e
                    y, gate = R["h"][:, 2 * u:2 * u + 2, :], R[name][:, 2 * u:2 * u + 2, :]
                    for j in range(2):
                        V.scalar_tensor_tensor(out=gate[:, j, :], in0=ps[:, j, :], scalar=col(bias, 2 * u + j),
                                                  in1=gate[:, j, :], op0=ALU.add, op1=ALU.mult).then_inc(vector_done, w.step(("evac", g)))
                    dve.wait_ge(vector_done, w.now())
                    V.tensor_tensor(y, y, gate, ALU.add).then_inc(vector_done, w.step())
                elif kind == "resid":
                    _, layer, at, u = e
                    for j in range(2):
                        x = R["x"][:, 2 * u + j, :]
                        V.scalar_tensor_tensor(out=x, in0=ps[:, j, :],
                                                  scalar=ada[:, layer % 2, at + 2 * u + j:at + 2 * u + j + 1], in1=x,
                                                  op0=ALU.mult, op1=ALU.add).then_inc(vector_done, w.step(("evac", g)))
                elif kind == "expert":
                    _, layer, at, u = e
                    x = R["x"][:, 2 * u:2 * u + 2, :]
                    tmp = R["weighted"]
                    comb = work[:, bass.ds(w.round * T + comb_off, T)]
                    dve.wait_ge(vector_done, w.now())
                    for j in range(2):
                        V.scalar_tensor_tensor(out=tmp[:, j, :], in0=ps[:, j, :],
                                                  scalar=ada[:, layer % 2, at + 2 * u + j:at + 2 * u + j + 1],
                                                  in1=comb, op0=ALU.mult, op1=ALU.mult).then_inc(vector_done, w.step())
                    dve.wait_ge(vector_done, w.now())
                    V.tensor_tensor(x, x, tmp, ALU.add).then_inc(vector_done, w.step(("evac", g)))

            def norm(it):
                begin(it)
                sq, t1, y, u = temps(it)
                nt, s = it["nt"], it["s"]
                dve.wait_ge(tensor_done, w.at("sums", s))
                nn = 1 if it["total"] else nt
                for b in range((nn + 1) // 2):
                    m = min(2, nn - 2 * b)
                    V.tensor_scalar(t1[:, 2 * b:2 * b + m, :],
                                       sbank(b)[:, 0:m * T].rearrange("p (a t) -> p a t", t=T), it["inv"], EPS, ALU.mult,
                                       ALU.add).then_inc(vector_done, w.step(("mean", s)))
                dve.wait_ge(scalar_done, w.at("root", s))
                yy, uu, tt = y[:, 0:nn, :], u[:, 0:nn, :], t1[:, 0:nn, :]
                V.tensor_tensor(uu, yy, yy, ALU.mult).then_inc(vector_done, w.step())
                dve.wait_ge(vector_done, w.now())
                V.tensor_tensor(uu, uu, tt, ALU.mult).then_inc(vector_done, w.step())
                dve.wait_ge(vector_done, w.now())
                V.tensor_scalar(uu, uu, -0.5 * it["const"], 1.5 * it["const"], ALU.mult, ALU.add).then_inc(vector_done, w.step())
                dve.wait_ge(vector_done, w.now())
                V.tensor_tensor(yy, yy, uu, ALU.mult).then_inc(vector_done, w.step())
                dve.wait_ge(vector_done, w.now())
                src, dst = R[it["src"]], R[it["dst"]]
                for t in range(nt):
                    if it["gain"] == "A":
                        gcol = acol[:, t:t + 1]
                    else:
                        gcol = col(it["gain"], t if colat[it["gain"]][1] > 1 else 0)
                    V.scalar_tensor_tensor(out=dst[:, t, :], in0=src[:, t, :], scalar=gcol,
                                              in1=y[:, 0 if it["total"] else t, :], op0=ALU.mult, op1=ALU.mult).then_inc(vector_done, w.step(("scaled_tile", s, t), ("scaled", s)))
                post = it["post"]
                if post and post[0] == "mul":
                    dve.wait_ge(vector_done, w.now())
                    V.tensor_tensor(dst[:, 0:nt, :], dst[:, 0:nt, :], R[post[1]][:, 0:nt, :], ALU.mult).then_inc(vector_done, w.step())
                if post and post[0] == "rope":
                    dve.wait_ge(vector_done, w.now())
                    d = dst[:, 0:nt, :]
                    cos = R["cos" + post[1]].to_broadcast([P, nt, T]) if nt > 1 else R["cos" + post[1]]
                    sin = R["sin" + post[1]].to_broadcast([P, nt, T]) if nt > 1 else R["sin" + post[1]]
                    dve.wait_ge(tensor_done, w.at("turned", s))
                    V.tensor_tensor(d, d, cos, ALU.mult).then_inc(vector_done, w.step())
                    for b in range((nt + 1) // 2):
                        m = min(2, nt - 2 * b)
                        V.tensor_tensor(t1[:, 2 * b:2 * b + m, :],
                                           sbank(2 + b)[:, 0:m * T].rearrange("p (a t) -> p a t", t=T),
                                           sin[:, 2 * b:2 * b + m, :] if nt > 1 else sin, ALU.mult).then_inc(vector_done, w.step())
                    dve.wait_ge(vector_done, w.now())
                    V.tensor_tensor(d, d, t1[:, 0:nt, :], ALU.add).then_inc(vector_done, w.step())

            def hg_prep(it):
                begin(it)
                s, z, e, qt = it["s"], R["z"], R["e"], R["qt"]
                if it["layer"] == 0:
                    V.scalar_tensor_tensor(out=e, in0=z, scalar=-1.0, in1=z, op0=ALU.mult, op1=ALU.max).then_inc(vector_done, w.step(("abs_z", s)))
                    dve.wait_ge(scalar_done, w.at("softplus", s))
                    V.scalar_tensor_tensor(out=qt, in0=z, scalar=0.0, in1=e, op0=ALU.min, op1=ALU.subtract).then_inc(vector_done, w.step())
                    dve.wait_ge(vector_done, w.now())
                else:
                    V.tensor_tensor(small[:, 8:12], col("a1_lb", 0, 4), col("a0_lb", 0, 4), ALU.subtract).then_inc(vector_done, w.step(("lb_in", s)))
                    dve.wait_ge(scalar_done, w.at("lb", s))
                    dve.wait_ge(scalar_done, w.at("kin", s))
                    V.tensor_scalar(small[:, 12:16], small[:, 8:12], -1.0, 1.0, ALU.mult, ALU.add).then_inc(vector_done, w.step())
                    dve.wait_ge(vector_done, w.now())
                    for h in range(4):
                        V.tensor_scalar(e[:, h, :], e[:, h, :], small[:, 12 + h:13 + h], small[:, 8 + h:9 + h],
                                           ALU.mult, ALU.add).then_inc(vector_done, w.step())
                        V.tensor_scalar(R["kin"][:, h, :], R["kin"][:, h, :], small[:, 12 + h:13 + h], None, ALU.mult).then_inc(vector_done, w.step())
                    dve.wait_ge(vector_done, w.now())
                    V.tensor_single_scalar(e, e, 2.0 ** -63, ALU.max).then_inc(vector_done, w.step(("forget", s)))
                    dve.wait_ge(scalar_done, w.at("log_f", s))
                for h in range(4):
                    V.tensor_tensor_scan(R["b"][:, h, :], con("ones"), qt[:, h, :], 0.0, ALU.mult, ALU.add).then_inc(vector_done, w.step())
                V.memset(R["sc"], 0.0).then_inc(vector_done, w.step())

            def hg_level(it):
                begin(it)
                n, s = it["level"], it["s"]
                flat = lambda name: R[name].rearrange("p a t -> p (a t)")
                sc = R["sc"]
                if n == 0:
                    w.mark("decayed", s)
                if n > 0:
                    b = flat("b").rearrange("p (m w) -> p m w", w=2 * n)
                    e = flat("e").rearrange("p (m w) -> p m w", w=2 * n)
                    ref = b[:, :, n - 1:n].to_broadcast([P, 4 * T // (2 * n), n])
                    V.tensor_tensor(e[:, :, 0:n], ref, b[:, :, 0:n], ALU.subtract).then_inc(vector_done, w.step())
                    V.tensor_tensor(e[:, :, n:2 * n], b[:, :, n:2 * n], ref, ALU.subtract).then_inc(vector_done, w.step(("spans", s)))
                    dve.wait_ge(scalar_done, w.at("decays", s))
                    V.tensor_tensor(R["qt"], R["q"], R["e"], ALU.mult).then_inc(vector_done, w.step())
                    V.tensor_tensor(R["kt"], R["kin"], R["e"], ALU.mult).then_inc(vector_done, w.step(("decayed", s)))
                dve.wait_ge(tensor_done, w.at("level", s))
                if n == 128:
                    V.tensor_copy(sc[:, 1, :], sbank(0)).then_inc(vector_done, w.step())
                else:
                    m = con("ident") if n == 0 else con("levels", P * LEVELS.index(n), P)
                    m = m.bitcast(I32).unsqueeze(1).to_broadcast([P, 4, P])
                    for t in range(2):
                        V.copy_predicated(sc[:, 2 * t, :].rearrange("p (h n) -> p h n", h=4), m,
                                             sbank(t).rearrange("p (h n) -> p h n", h=4)).then_inc(vector_done, w.step())

            def attn(it):
                begin(it)
                soft_s, soft_w, turned = soft(it)
                what, s = it["what"], it["s"]
                if it["out"]:
                    i, q = it["out"]
                    dve.wait_ge(tensor_done, w.at("attn_out", s))
                    dst = R[{"diff": "dq", "moba": "mq", "mla": "qn"}[what]][:, i, q * P:(q + 1) * P]
                    if what == "diff":
                        V.tensor_copy(dst, sbank(3)[:, 0:P]).then_inc(vector_done, w.step())
                    else:
                        V.tensor_copy(dst[0:64, :], sbank(3)[0:64, 0:P]).then_inc(vector_done, w.step())
                        V.tensor_copy(dst[64:128, :], sbank(3)[64:128, P:2 * P]).then_inc(vector_done, w.step())
                if it["load"]:
                    i, q = it["load"]
                    n = (q + 1) * P
                    k0 = T - n
                    dve.wait_ge(tensor_done, w.at("scores", s))
                    scale = {"diff": 64 ** -0.5, "moba": 64 ** -0.5, "mla": 96 ** -0.5}[what]
                    bias = con("alibi", T * i + k0, n) if what == "diff" else con("mask", k0, n)
                    V.scalar_tensor_tensor(out=soft_s[:, :, 0:n],
                                              in0=psum[:, GBANKS:GBANKS + 2, 0:n],
                                              scalar=scale, in1=bias.unsqueeze(1).to_broadcast([P, 2, n]),
                                              op0=ALU.mult, op1=ALU.add).then_inc(vector_done, w.step())
                    dve.wait_ge(vector_done, w.now())
                    V.tensor_reduce(small[:, 20:22], soft_s[:, :, 0:n], AX.X, ALU.max).then_inc(vector_done, w.step())
                    dve.wait_ge(vector_done, w.now())
                    V.tensor_single_scalar(small[:, 22:24], small[:, 20:22], -1.0, ALU.mult).then_inc(vector_done, w.step(("neg_max", s)))
                    dve.wait_ge(scalar_done, w.at("exps", s))
                    V.reciprocal(small[:, 26:28], small[:, 24:26]).then_inc(vector_done, w.step())
                    dve.wait_ge(vector_done, w.now())
                    dve.wait_ge(tensor_done, w.at("attn_turn", s))
                    if what == "diff":
                        V.tensor_scalar(small[:, 28:29], small[:, 27:28], small[:, 5:6], None, ALU.mult).then_inc(vector_done, w.step())
                        dve.wait_ge(vector_done, w.now())
                        V.tensor_scalar(soft_s[:, 1, 0:n], soft_s[:, 1, 0:n], small[:, 28:29], None, ALU.mult).then_inc(vector_done, w.step())
                        dve.wait_ge(vector_done, w.now())
                        V.scalar_tensor_tensor(out=soft_w[:, 0, 0:n], in0=soft_s[:, 0, 0:n], scalar=small[:, 26:27],
                                                  in1=soft_s[:, 1, 0:n], op0=ALU.mult, op1=ALU.add).then_inc(vector_done, w.step())
                    else:
                        for c in range(2):
                            V.tensor_scalar(soft_w[:, c, 0:n], soft_s[:, c, 0:n], small[:, 26 + c:27 + c], None,
                                               ALU.mult).then_inc(vector_done, w.step())

            def router(it):
                begin(it)
                s = it["s"]
                L = small[:, 48:64].rearrange("p (t e) -> p t e", t=2)
                E = small[:, 64:80].rearrange("p (t e) -> p t e", t=2)
                dve.wait_ge(tensor_done, w.at("logits", s))
                V.tensor_copy(L, sbank(0)[:, 0:16].rearrange("p (t e) -> p t e", t=2)).then_inc(vector_done, w.step())
                dve.wait_ge(vector_done, w.now())
                V.tensor_reduce(small[:, 80:82], L, AX.X, ALU.max).then_inc(vector_done, w.step())
                dve.wait_ge(vector_done, w.now())
                V.tensor_single_scalar(small[:, 82:84], small[:, 80:82], -1.0, ALU.mult).then_inc(vector_done, w.step(("neg_max", s)))
                big = work[:, hb + 2048:hb + 2048 + 256]
                gt = big[:, 0:128].rearrange("p (t e j) -> p t e j", t=2, e=8)
                eq = big[:, 128:256].rearrange("p (t e j) -> p t e j", t=2, e=8)
                for t in range(2):
                    lj = L[:, t, :].unsqueeze(1).to_broadcast([P, 8, 8])
                    le = L[:, t, :].unsqueeze(2).to_broadcast([P, 8, 8])
                    V.tensor_tensor(gt[:, t], lj, le, ALU.is_gt).then_inc(vector_done, w.step())
                    V.tensor_tensor(eq[:, t], lj, le, ALU.is_equal).then_inc(vector_done, w.step())
                dve.wait_ge(vector_done, w.now())
                for t in range(2):
                    V.tensor_tensor(eq[:, t], eq[:, t], con("before").rearrange("p (e j) -> p e j", e=8), ALU.mult).then_inc(vector_done, w.step())
                dve.wait_ge(vector_done, w.now())
                V.tensor_tensor(big[:, 0:128], big[:, 0:128], big[:, 128:256], ALU.add).then_inc(vector_done, w.step())
                dve.wait_ge(vector_done, w.now())
                for t in range(2):
                    V.tensor_reduce(small[:, 88 + 8 * t:96 + 8 * t], gt[:, t], AX.X, ALU.add).then_inc(vector_done, w.step())
                dve.wait_ge(vector_done, w.now())
                V.tensor_single_scalar(small[:, 88:104], small[:, 88:104], 2.0, ALU.is_lt).then_inc(vector_done, w.step())
                dve.wait_ge(vector_done, w.now())
                dve.wait_ge(scalar_done, w.at("exps", s))
                V.tensor_tensor(small[:, 64:80], small[:, 64:80], small[:, 88:104], ALU.mult).then_inc(vector_done, w.step())
                dve.wait_ge(vector_done, w.now())
                V.tensor_reduce(small[:, 84:86], E, AX.X, ALU.add).then_inc(vector_done, w.step())
                dve.wait_ge(vector_done, w.now())
                V.reciprocal(small[:, 86:88], small[:, 84:86]).then_inc(vector_done, w.step())
                dve.wait_ge(vector_done, w.now())
                for t in range(2):
                    V.tensor_scalar(E[:, t, :], E[:, t, :], small[:, 86 + t:87 + t], None, ALU.mult).then_inc(vector_done, w.step())
                dve.wait_ge(vector_done, w.now())
                dg = region(hb, 8)
                for e in range(EXPERTS):
                    for t in range(2):
                        V.tensor_scalar(dg[:, e, t * P:(t + 1) * P], con("ident"), E[:, t, e:e + 1], None, ALU.mult).then_inc(vector_done, w.step(("diagonals", s)))
                dve.wait_ge(tensor_done, w.at("comb", s))
                for b in range(4):
                    V.tensor_copy(R["comb"][:, 2 * b:2 * b + 2, :], sbank(b).rearrange("p (a t) -> p a t", t=T)).then_inc(vector_done, w.step())

            def rope_tables(it):
                begin(it)
                s = it["s"]
                tmp = temps(it)[0]
                posf, turns, ang = tmp[:, 1, :], tmp[:, 2, :], tmp[:, 3, :]
                dve.wait_ge(inputs_loaded, w.at("inputs"))
                V.tensor_copy(posf, pos[:, :]).then_inc(vector_done, w.step())
                magic = 1.5 * 2.0 ** 23
                c1, c2 = 6.28125, float(np.float32(int(0.0019353071795864769 * 2 ** 21) / 2 ** 21))
                c3 = 2 * math.pi - c1 - c2
                for j, name in enumerate(("64", "32")):
                    dve.wait_ge(vector_done, w.now())
                    V.tensor_scalar(ang, posf, con("freq" + name), None, ALU.mult).then_inc(vector_done, w.step())
                    dve.wait_ge(vector_done, w.now())
                    V.tensor_scalar(turns, ang, 1.0 / (2 * math.pi), magic, ALU.mult, ALU.add).then_inc(vector_done, w.step())
                    dve.wait_ge(vector_done, w.now())
                    V.tensor_single_scalar(turns, turns, magic, ALU.subtract).then_inc(vector_done, w.step())
                    for c in (c1, c2, c3):
                        dve.wait_ge(vector_done, w.now())
                        V.scalar_tensor_tensor(out=ang, in0=turns, scalar=-c, in1=ang, op0=ALU.mult, op1=ALU.add).then_inc(vector_done, w.step())
                    dve.wait_ge(vector_done, w.now())
                    V.tensor_scalar(R["cos" + name][:, 0, :], ang, 3.1415925, -3.1415925, ALU.min, ALU.max).then_inc(vector_done, w.step(("angle", s, j)))
                    dve.wait_ge(scalar_done, w.at("half", s, j))
                    cos = R["cos" + name][:, 0, :]
                    V.tensor_tensor(cos, cos, cos, ALU.mult).then_inc(vector_done, w.step())
                    dve.wait_ge(vector_done, w.now())
                    V.tensor_scalar(cos, cos, -2.0, 1.0, ALU.mult, ALU.add).then_inc(vector_done, w.step())
                V.memset(R["cu"][:, :, 0:CONV_W - 1], 0.0).then_inc(vector_done, w.step())

            def run(steps):
                for it in steps:
                    kind = it["kind"]
                    if kind == "unit":
                        unit(it)
                    elif kind == "fence":
                        fence(it)
                    elif kind == "end":
                        pass
                    elif kind == "ada":
                        n = it["n"]
                        dve.wait_ge(tensor_done, w.at("ada_sum", n))
                        if n == 0:
                            dve.wait_ge(inputs_loaded, w.at("inputs"))
                        pre = ("a0", "a1", "b0", "b1")[it["layer"]]
                        V.tensor_tensor(ada[:, it["layer"] % 2, 2 * it["a"]:2 * it["a"] + 2], ada_bank[:, 0:2],
                                           col(pre + "_mod_b", 2 * it["a"], 2), ALU.add).then_inc(vector_done, w.step(("ada", n)))
                    else:
                        if kind == "norm":
                            norm(it)
                        elif kind == "modcols":
                            begin(it)
                            dve.wait_ge(vector_done, w.now())
                            sc = ada[:, it["layer"] % 2, it["scale"]:it["scale"] + 8]
                            V.scalar_tensor_tensor(out=acol[:, :], in0=sc, scalar=1.0, in1=col(it["gain"], 0, 8),
                                                      op0=ALU.add, op1=ALU.mult).then_inc(vector_done, w.step())
                            dve.wait_ge(vector_done, w.now())
                        elif kind == "hg_prep":
                            hg_prep(it)
                        elif kind == "hg_level":
                            hg_level(it)
                        elif kind == "attn":
                            attn(it)
                        elif kind == "lam":
                            begin(it)
                            l, s = it["layer"], it["s"]
                            lam = col(f"a{l}_lam", 0, 4).rearrange("p (a b) -> p a b", b=2)
                            V.tensor_tensor(small[:, 0:2], lam[:, :, 0], lam[:, :, 1], ALU.mult).then_inc(vector_done, w.step(("lam_products", s)))
                            dve.wait_ge(scalar_done, w.at("lam_exps", s))
                            V.tensor_tensor(small[:, 4:5], small[:, 3:4], small[:, 2:3], ALU.subtract).then_inc(vector_done, w.step())
                            dve.wait_ge(vector_done, w.now())
                            V.tensor_single_scalar(small[:, 5:6], small[:, 4:5], -LAM_INIT[l], ALU.add).then_inc(vector_done, w.step())
                            dve.wait_ge(vector_done, w.now())
                        elif kind == "conv":
                            begin(it)
                            t, l = it["tile"], it["layer"]
                            dve.wait_ge(vector_done, w.at("conv_gate_used", it["needs"][0][1]))
                            dve.wait_ge(vector_done, w.now())
                            y = R["ca"][:, t, :]
                            for tap in range(CONV_W):
                                u = R["cu"][:, t, tap:tap + T]
                                wcol = col(f"b{l}_dw_w", tap * 4 + t)
                                if tap == 0:
                                    V.tensor_scalar(y, u, wcol, col(f"b{l}_dw_b", t), ALU.mult, ALU.add).then_inc(vector_done, w.step())
                                else:
                                    V.scalar_tensor_tensor(out=y, in0=u, scalar=wcol, in1=y, op0=ALU.mult, op1=ALU.add).then_inc(vector_done, w.step())
                                dve.wait_ge(vector_done, w.now())
                        elif kind == "center":
                            begin(it)
                            dve.wait_ge(tensor_done, w.at("center", it["s"]))
                            mu = temps(it)[1][:, 0:1, :]
                            V.tensor_scalar(mu, sbank(0)[:, 0:T].unsqueeze(1), 1.0 / 512, None, ALU.mult).then_inc(vector_done, w.step())
                            dve.wait_ge(vector_done, w.now())
                            V.tensor_tensor(R["ca"], R["ca"], mu.to_broadcast([P, 4, T]), ALU.subtract).then_inc(vector_done, w.step())
                            dve.wait_ge(vector_done, w.now())
                        elif kind == "router":
                            router(it)
                        elif kind == "rope_tables":
                            rope_tables(it)
                        w.mark("side", it["s"], w.name)

            run(before)
            if experts:
                with dve.Fori(0, EXPERTS) as e:
                    w.begin_rounds(e)
                    run(experts)
                    w.end_rounds()
            run(after)

        @block.gpsimd
        def _(pool):
            w = Count("POOL", book)
            G = nc.gpsimd
            steps = [it for it in plan if it["kind"] == "ada"]

            def load(k):
                if k < len(steps):
                    it = steps[k]
                    pool.wait_ge(gpsimd_done, w.now())
                    pool.dma_start(mod_in[:, k % 2, :], arrays["mods"][it["layer"], it["a"]]).then_inc(
                        mod_loaded[k % 2], w.step(("mod_in", k), of=f"mod{k % 2}", by=16))

            load(0)
            load(1)
            pool.wait_ge(scalar_done, w.at("silu_c"))
            for k, it in enumerate(steps):
                buf = mod_in[:, k % 2, :]
                b3 = buf.rearrange("p (k n) -> p k n", k=DK)
                cvec = act_c[:, it["layer"] // 2, :].unsqueeze(2).to_broadcast([P, DK, 256])
                pool.wait_ge(mod_loaded[k % 2], w.at("mod_in", k))
                G.tensor_tensor(b3, b3, cvec, ALU.mult).then_inc(gpsimd_done, w.step())
                for h in (1024, 512):
                    pool.wait_ge(gpsimd_done, w.now())
                    G.tensor_tensor(buf[:, 0:h], buf[:, 0:h], buf[:, h:2 * h], ALU.add).then_inc(gpsimd_done, w.step())
                pool.wait_ge(gpsimd_done, w.now())
                if k >= ACCS:
                    pool.wait_ge(tensor_done, w.at("ada_sum", k - ACCS))
                G.tensor_tensor(mod_acc[:, k % ACCS, :], buf[:, 0:256], buf[:, 256:512], ALU.add).then_inc(gpsimd_done, w.step(("mod_acc", k)))
                load(k + 2)


def lay_out(i):
    def tiles(w, cols):
        k, n = w.shape
        return w.reshape(k // P, P, n // cols, cols).transpose(2, 1, 0, 3).reshape(n // cols, P, -1)

    def column(v):
        return v.reshape(-1, P).T

    def twice(v, n):
        return np.tile(v, n)[:, None]

    a = {}
    x = i["x"][0]
    a["xT"] = x.T.reshape(8, P, T).transpose(1, 0, 2)
    a["mods"] = np.stack([tiles(w, 256) for w in (*i["ada_w"], *i["w_mod_2"])])
    a["w_in1"] = np.stack([tiles(w, 512) for w in i["w_in"]])
    a["w_pa"] = np.stack([tiles(w, 1024)[0] for w in i["w_branch_a"]])
    a["w_pb"] = np.stack([tiles(w, 1024)[0] for w in i["w_branch_b"]])
    a["w_o1"] = np.stack([tiles(w, 512) for w in i["w_out"]])

    def pairs(w1, w3):
        n = w1.shape[1] // 256
        both = np.stack([w1.reshape(D, n, 256), w3.reshape(D, n, 256)], 2).reshape(D, n * 512)
        return tiles(both, 512)

    def halves(w):
        k, n = w.shape
        kt = k // P
        return w.reshape(2, kt // 2, P, 4, 256).transpose(3, 0, 2, 1, 4).reshape(4, 2, P, -1)

    a["f13"] = pairs(i["ffn_w1"][0], i["ffn_w3"][0])
    a["f2"] = halves(i["ffn_w2"][0])
    a["m13"] = np.stack([pairs(w1, w3) for w1, w3 in zip(i["moe_w1"][0], i["moe_w3"][0])])
    a["m2"] = np.stack([halves(w) for w in i["moe_w2"][0]])
    w = i["w_in_2"]
    lat = np.concatenate([w[:, :, :640], np.tile(w[:, :, 640:672], (1, 1, 4))], 2)
    main = np.concatenate([lat[:, :, :512], w[:, :, 672:]], 2)
    a["w_in2"] = np.stack([tiles(x, 512) for x in main])
    a["w_in2x"] = np.stack([tiles(np.ascontiguousarray(x[:, 512:]), 256)[0] for x in lat])
    uq = i["w_uq_2"].reshape(2, 384, 8, 96)
    a["w_uq"] = np.stack([tiles(np.concatenate([u[:, :, :64].reshape(384, 512), u[:, :, 64:].reshape(384, 256)], 1), 768)[0]
                          for u in uq])
    ukv = i["w_ukv_2"].reshape(2, 256, 8, 128)
    a["w_ukv"] = np.stack([tiles(np.concatenate([u[:, :, :64].reshape(256, 512), u[:, :, 64:].reshape(256, 512)], 1), 1024)[0]
                           for u in ukv])
    for name, key in (("w_mla", "w_mla_o_2"), ("w_moba", "w_moba_o_2"), ("w_pw", "w_conv_pw2_2")):
        a[name] = np.stack([tiles(w, 1024)[0] for w in i[key]])
    a["w_o2"] = np.stack([tiles(w, 512) for w in i["w_out_2"]])
    a["up"] = np.stack([pairs(w[:, :D_FF], w[:, D_FF:]) for w in i["w_up_2"]])
    a["down"] = np.stack([halves(w) for w in i["w_down_2"]])
    a["positions"] = i["positions_2"].reshape(1, T)
    at, n = column_map()
    c = np.zeros((P, n), np.float32)

    def put(name, value):
        o, wd = at[name]
        c[:, o:o + wd] = value

    put("c1", column(i["c"][0]))
    put("c2", column(i["c_2"][0]))
    for l in range(2):
        put(f"a{l}_mix_g", column(i["norm_mix_g"][l]))
        put(f"a{l}_ffn_g", column(i["norm_ffn_g"][l]))
        put(f"a{l}_lb", column(i["hgrn_lb_logits"][l]))
        put(f"a{l}_hg_g", column(i["hgrn_norm_g"][l]))
        put(f"a{l}_qn_g", twice(i["da_qnorm_g"][l], 2))
        put(f"a{l}_kn_g", twice(i["da_knorm_g"][l], 2))
        put(f"a{l}_lam", np.tile(i["da_lambda"][l].T, (2, 1)))
        put(f"a{l}_sub_g", column(i["da_subln_g"][l]))
        put(f"a{l}_mod_b", column(i["ada_b"][l]))
        put(f"b{l}_mix_g", column(i["mix_norm_g_2"][l]))
        put(f"b{l}_ffn_g", column(i["ffn_norm_g_2"][l]))
        put(f"b{l}_mod_b", column(i["b_mod_2"][l]))
        put(f"b{l}_ql_g", column(i["mla_q_norm_g_2"][l]))
        put(f"b{l}_kl_g", column(i["mla_kv_norm_g_2"][l]))
        put(f"b{l}_qn_g", twice(i["mla_qn_nope_g_2"][l], 2))
        put(f"b{l}_qr_g", twice(i["mla_qn_rope_g_2"][l], 4))
        put(f"b{l}_kn_g", twice(i["mla_kn_nope_g_2"][l], 2))
        put(f"b{l}_kr_g", twice(i["mla_kn_rope_g_2"][l], 4))
        put(f"b{l}_bq_g", twice(i["moba_qn_g_2"][l], 2))
        put(f"b{l}_bk_g", twice(i["moba_kn_g_2"][l], 2))
        put(f"b{l}_dw_w", i["conv_dw_w_2"][l].reshape(CONV_W, 4, P).transpose(2, 0, 1).reshape(P, -1))
        put(f"b{l}_dw_b", column(i["conv_dw_b_2"][l]))
        put(f"b{l}_ln_g", column(i["conv_ln_g_2"][l]))
        put(f"b{l}_ln_b", column(i["conv_ln_b_2"][l]))
        put(f"b{l}_pw_b", column(i["b_conv_pw2_2"][l]))
        put(f"b{l}_fw", i["ffn_dw_w_2"][l].reshape(3, 44, P).transpose(2, 0, 1).reshape(P, -1))
        put(f"b{l}_fb", column(i["ffn_dw_b_2"][l]))
    put("router", i["moe_router"][0].reshape(DK, P, 8).transpose(1, 0, 2).reshape(P, 64))
    a["columns"] = c
    a["constants"] = constants()
    return {k: np.ascontiguousarray(v) for k, v in a.items()}


def program(bacc, shapes, book):
    nc = bacc.Bacc("TRN2", target_bir_lowering=False, num_devices=1)
    aps = {k: nc.dram_tensor("in_" + k, s, d, kind="ExternalInput").ap() for k, (s, d) in shapes.items()}
    out = nc.dram_tensor("xT_out", (P, 8, T), F32, kind="ExternalOutput").ap()
    build(nc, aps, out, book, aps["columns"], aps["constants"])
    return nc


def kernel(**inputs):
    import concourse.bacc as bacc
    from concourse.bass_utils import run_bass_kernel_spmd
    arrays = lay_out({k: np.asarray(v) for k, v in inputs.items()})
    shapes = {k: (v.shape, mybir.dt.from_np(v.dtype)) for k, v in arrays.items()}
    book = Book()
    program(bacc, shapes, book)
    book.known = book.at
    nc = program(bacc, shapes, book)
    r = run_bass_kernel_spmd(nc, [{"in_" + k: v for k, v in arrays.items()}], core_ids=[0])
    y = r.results[0]["xT_out"]
    return np.ascontiguousarray(y.transpose(2, 1, 0).reshape(1, T, D))
```

```python
from contextlib import ExitStack
import math

import numpy as np
import concourse.bass as bass
from concourse import mybir

ALU = mybir.AluOpType
ACT = mybir.ActivationFunctionType
F32 = mybir.dt.float32
I32 = mybir.dt.int32
AX = mybir.AxisListType

P = 128
T = 256
D = 1024
DK = D // P
EPS = 1e-6
D_FF = 2816
FF_U = D_FF // 256
D_FE = 3584
FE_U = D_FE // 256
EXPERT_CHUNKS = FE_U + 8
ROUND_BANKS = FE_U + 8
EXPERTS = 8
CONV_W = 31
RING = 4
SLOT = 4096
MODW = 2048
ACCS = 4
GBANKS = 3
NEG = -1.0e30
LEVELS = (1, 2, 4, 8, 16, 32, 64)
LAM_INIT = [0.8 - 0.6 * math.exp(-0.3 * l) for l in range(2)]


def column_map():
    at, n = {}, 0

    def put(name, width):
        nonlocal n
        at[name] = (n, width)
        n += width

    put("c1", 8)
    put("c2", 8)
    for l in range(2):
        for name, width in (("mix_g", 8), ("ffn_g", 8), ("lb", 4), ("hg_g", 1), ("qn_g", 1), ("kn_g", 1), ("lam", 4),
                            ("sub_g", 1), ("mod_b", 48)):
            put(f"a{l}_{name}", width)
    put("router", 64)
    for l in range(2):
        for name, width in (("mix_g", 8), ("ffn_g", 8), ("mod_b", 48), ("ql_g", 3), ("kl_g", 2), ("qn_g", 1),
                            ("qr_g", 1), ("kn_g", 1), ("kr_g", 1), ("bq_g", 1), ("bk_g", 1), ("dw_w", 4 * CONV_W),
                            ("dw_b", 4), ("ln_g", 4), ("ln_b", 4), ("pw_b", 8), ("fw", 132), ("fb", 44)):
            put(f"b{l}_{name}", width)
    return at, n


def constant_map():
    at, n = {}, 0

    def put(name, width):
        nonlocal n
        at[name] = (n, width)
        n += width

    for name, width in (("ident", 128), ("ones", 256), ("blk64", 128), ("blk32", 128), ("rot64", 128),
                        ("rot32", 128), ("mask", 256), ("levels", 128 * len(LEVELS)), ("alibi", 4 * 256),
                        ("before", 64), ("earlier", 128), ("slots", 128), ("freq64", 1), ("freq32", 1)):
        put(name, width)
    return at, n


def constants():
    at, n = constant_map()
    c = np.zeros((P, n), np.float32)
    p, f = np.arange(P)[:, None], np.arange(P)[None, :]

    def put(name, value):
        o, w = at[name]
        c[:, o:o + w] = value

    put("ident", p == f)
    put("ones", 1.0)
    put("blk64", p // 64 == f // 64)
    put("blk32", p // 32 == f // 32)
    for w in (64, 32):
        h = w // 2
        same = p // w == f // w
        put(f"rot{w}", np.where(same & (p == f + h), -1.0, 0.0) + np.where(same & (p == f - h), 1.0, 0.0))
    dist = (P + p - np.arange(T)[None, :]).astype(np.float32)
    put("mask", np.where(dist < 0, NEG, 0.0))
    put("levels", np.concatenate([(p // (2 * s) == f // (2 * s)) & (p % (2 * s) < s) & (f % (2 * s) >= s)
                                  for s in LEVELS], 1))
    put("alibi", np.concatenate([np.where(dist < 0, NEG, -np.float32(2.0 ** (-8.0 * (h + 1) / 4)) * dist)
                                 for h in range(4)], 1))
    e, j = np.arange(8)[:, None], np.arange(8)[None, :]
    put("earlier", p < f)
    put("slots", np.arange(P, dtype=np.float32)[None, :])
    put("before", (j < e).astype(np.float32).reshape(1, 64))
    for name, w in (("freq64", 64), ("freq32", 32)):
        inv = (1.0 / (np.float32(10000.0) ** (np.arange(0, w, 2, dtype=np.float32) / np.float32(w)))).astype(np.float32)
        put(name, inv[np.arange(P) % (w // 2)][:, None])
    return c


def make_plan():
    plan, state = [], {"chunk": 0, "bank": 0, "side": 0, "ada": 0, "fence": 0}

    def chunk(name, idx, width):
        c = dict(id=(name,) + tuple(idx), n=state["chunk"], slot=state["chunk"] % RING, name=name, idx=idx, width=width)
        state["chunk"] += 1
        return c

    def unit(parts, rhs, evac, load, free, mode="F", tile=0, ready=(), after=()):
        u = dict(kind="unit", g=state["bank"], bank=state["bank"] % GBANKS, parts=parts, rhs=rhs, evac=evac,
                 load=load, free=free, mode=mode, tile=tile, ready=ready, after=after)
        state["bank"] += 1
        return u

    def side(kind, **kw):
        s = {"kind": kind, "s": state["side"], "needs": [], **kw}
        state["side"] += 1
        return s

    def fence():
        state["fence"] += 1
        return dict(kind="fence", n=state["fence"])

    def adas(layer, lo, hi):
        out = []
        for a in range(lo, hi):
            out.append(dict(kind="ada", n=state["ada"], layer=layer, a=a))
            state["ada"] += 1
        return out

    def f_units(name, idx, kt, cols, rhs, evacs, ready=()):
        c = chunk(name, idx, kt * cols)
        n = len(evacs)
        return [unit([(c, kt, cols, 256 * j, 0)], rhs, evacs[j], [c] if j == 0 else [], [c] if j == n - 1 else [],
                     ready=ready) for j in range(n)]

    def t_units(c, kt, cols, col, rhs, evacs, load, ready=()):
        return [unit([(c, kt, cols, col, 0)], rhs, evacs[t], load if t == 0 else [], [c] if t == 1 else [], mode="T",
                     tile=t, ready=ready) for t in range(2)]

    def merge(units, sides, lead=0, every=1):
        out, i = [], 0
        for n, u in enumerate(units):
            out.append(u)
            if n >= lead and (n - lead) % every == 0 and i < len(sides):
                out.append(sides[i])
                i += 1
        return out + sides[i:]

    def spread(items, extra, every):
        out, i, n = [], 0, 0
        for it in items:
            out.append(it)
            n += it["kind"] == "unit"
            if it["kind"] == "unit" and n % every == 0 and i < len(extra):
                out.append(extra[i])
                i += 1
        return out + extra[i:]

    def norm(src, nt, gain, dst, inv, total=False, mat="ones", const=1.0, post=None, needs=()):
        return side("norm", src=src, nt=nt, gain=gain, dst=dst, inv=inv, total=total, mat=mat, const=const,
                    post=post, needs=list(needs))

    def modulate(layer, pre, gname, shift, scale):
        return side("modcols", gain=f"{pre}_{gname}", shift=shift, scale=scale, layer=layer), \
            norm("x", 8, "A", "h", 1.0 / D, total=True, post=("shift", layer, shift))

    def attention(kind, v):
        steps = [(i, q) for i in range(4) for q in range(2)]
        return [side("attn", what=kind, v=v, load=steps[n] if n < 8 else None,
                     turn=steps[n - 1] if 0 <= n - 1 < 8 else None, out=steps[n - 2] if n >= 2 else None, needs=[])
                for n in range(10)]

    def with_needs(items, keys):
        items[0].setdefault("needs", [])
        items[0]["needs"] = list(items[0]["needs"]) + list(keys)
        return items

    def evac(kind, *args):
        return (kind,) + args

    def glu_units(name, pre, nu, evacs):
        out = []
        for i in range(nu):
            c = chunk(name, pre + (i,), SLOT)
            ea, eb = evacs(i)
            out.append(unit([(c, DK, 512, 0, 0)], "h", ea, [c], []))
            out.append(unit([(c, DK, 512, 256, 0)], "h", eb, [], [c]))
        return out

    def down_units(name, pre, kt, rhs, evacs):
        out, half, ready = [], kt // 2, [("evac", state["bank"] - 1)]
        for i in range(4):
            cs = [chunk(name, pre + (i, k), half * 256) for k in range(2)]
            out.append(unit([(cs[0], half, 256, 0, 0), (cs[1], half, 256, 0, half)], rhs, evacs(i), cs, cs,
                            ready=ready))
        return out

    plan.append(side("start", needs=[]))
    plan.extend(adas(0, 0, 8))
    for l in range(2):
        pre = f"a{l}"
        if l == 0:
            rest = adas(0, 8, 24)
        else:
            rest = adas(2, 0, 24)
        plan.extend(modulate(l, pre, "mix_g", 0, 8))
        plan.append(fence())
        w = "w_in1"
        q = f_units(w, (l, 0), DK, 512, "h", [evac("act", "Copy", "q", u) for u in range(2)])
        z = f_units(w, (l, 1), DK, 512, "h", [evac("act", "Copy", "z", u) for u in range(2)])
        cv = chunk(w, (l, 2), SLOT)
        v = t_units(cv, DK, 512, 0, "h", [evac("act", "Copy", "v", u) for u in range(2)], [cv])
        hg = f_units(w, (l, 3), DK, 512, "h", [evac("act", "Silu", "hg", u) for u in range(2)])
        dq = f_units(w, (l, 4), DK, 512, "h", [evac("act", "Copy", "dq", u) for u in range(2)])
        dk = f_units(w, (l, 5), DK, 512, "h", [evac("act", "Copy", "dk", u) for u in range(2)])
        cd = chunk(w, (l, 6), SLOT)
        dv = t_units(cd, DK, 512, 0, "h", [evac("act", "Copy", "dv", u) for u in range(2)], [cd])
        gates = []
        for i in range(4):
            gates += f_units(w, (l, 7 + i), DK, 512, "h",
                             [evac("act", "Sigmoid", "ga" if i < 2 else "gb", 2 * (i % 2) + u) for u in range(2)])
        sides = [side("hg_prep", layer=l, needs=[("evac", z[1]["g"])])]
        sides += [side("hg_level", level=n, needs=[]) for n in (0,) + LEVELS + (128,)]
        sides += [side("hg_out", needs=[("evac", v[1]["g"])])]
        sides += [norm("z", 4, f"{pre}_hg_g", "z", 1.0 / 128, post=("mul", "hg"), needs=[("evac", hg[1]["g"])])]
        sides += [norm("dq", 4, f"{pre}_qn_g", "dq", 1.0 / 64, mat="blk64", needs=[("evac", dk[1]["g"])])]
        sides += [norm("dk", 4, f"{pre}_kn_g", "dk", 1.0 / 64, mat="blk64"), side("lam", layer=l, needs=[])]
        sides += with_needs(attention("diff", "dv"), [("evac", dv[1]["g"])])
        sides += [norm("dq", 4, f"{pre}_sub_g", "dq", 1.0 / 128, const=1.0 - LAM_INIT[l])]
        items = merge(q + z + v + hg + dq + dk + dv + gates, sides, lead=4)
        plan.extend(spread(items, rest, 1))
        plan.append(fence())
        items = f_units("w_pa", (l,), 4, 1024, "z", [evac("gate", "ga", u, 0) for u in range(4)])
        items += f_units("w_pb", (l,), 4, 1024, "dq", [evac("gate", "gb", u, 1) for u in range(4)])
        plan.extend(items)
        plan.append(fence())
        for i in range(2):
            plan.extend(f_units("w_o1", (l, i), DK, 512, "h", [evac("resid", l, 16, 2 * i + u) for u in range(2)]))
        plan.append(fence())
        plan.extend(modulate(l, pre, "ffn_g", 24, 32))
        if l == 0:
            plan.append(fence())
            items = glu_units("f13", (), FF_U, lambda i: (evac("glu_a", i), evac("glu_b", i)))
            plan.extend(spread(items, adas(1, 0, 24), 1))
            plan.append(fence())
            plan.extend(down_units("f2", (), 22, "hid", lambda i: evac("resid", l, 40, i)))
            plan.append(fence())
        else:
            plan.append(side("router", needs=[]))
            plan.append(fence())
            plan.append(dict(kind="experts"))
            plan.append(fence())

    for l in range(2):
        pre, L = f"b{l}", 2 + l
        plan.extend(modulate(L, pre, "mix_g", 0, 8))
        if l == 0:
            plan.append(side("rope_tables", needs=[]))
        plan.append(fence())
        w = "w_in2"
        lat = f_units(w, (l, 0), DK, 512, "h", [evac("act", "Copy", "lat", u) for u in range(2)])
        lat += f_units("w_in2x", (l,), DK, 256, "h", [evac("act", "Copy", "lat", 2)])
        mq = f_units(w, (l, 1), DK, 512, "h", [evac("act", "Copy", "mq", u) for u in range(2)])
        mk = f_units(w, (l, 2), DK, 512, "h", [evac("act", "Copy", "mk", u) for u in range(2)])
        cv = chunk(w, (l, 3), SLOT)
        mv = t_units(cv, DK, 512, 0, "h", [evac("act", "Copy", "mv", u) for u in range(2)], [cv])
        ca = f_units(w, (l, 4), DK, 512, "h", [evac("conv_in", "Copy", u) for u in range(2)])
        cg = f_units(w, (l, 5), DK, 512, "h", [evac("conv_in", "Sigmoid", u) for u in range(2)])
        gates = []
        for i in range(6):
            gates += f_units(w, (l, 6 + i), DK, 512, "h",
                             [evac("act", "Sigmoid", "gates", 2 * i + u) for u in range(2)])
        gates[-1]["after"] = [("conv_gate_used", cg[1]["g"])]
        lat_norms = [norm("ql", 3, f"{pre}_ql_g", "ql", 1.0 / 384, total=True, needs=[("evac", lat[2]["g"])]),
                     norm("kl", 2, f"{pre}_kl_g", "kl", 1.0 / 256, total=True)]
        ready = [("side_done", s["s"]) for s in lat_norms]
        uq = f_units("w_uq", (l,), 3, 768, "ql",
                     [evac("act", "Copy", "qn", 0), evac("act", "Copy", "qn", 1), evac("act", "Copy", "qp", 0)],
                     ready=ready)
        ck = chunk("w_ukv", (l,), 2 * 1024)
        kn = [unit([(ck, 2, 1024, 256 * j, 0)], "kl", evac("act", "Copy", "kn", j), [ck] if j == 0 else [], [],
                   ready=ready) for j in range(2)]
        va = t_units(ck, 2, 1024, 512, "kl", [evac("act", "Copy", "va", u) for u in range(2)], [], ready=ready)
        sides = lat_norms
        sides += [norm("kr", 1, f"{pre}_kr_g", "kr", 1.0 / 32, mat="blk32", post=("rope", "32"))]
        sides += [norm("mq", 4, f"{pre}_bq_g", "mq", 1.0 / 64, mat="blk64", post=("rope", "64"),
                       needs=[("evac", mk[1]["g"])]),
                  norm("mk", 4, f"{pre}_bk_g", "mk", 1.0 / 64, mat="blk64", post=("rope", "64"))]
        moba = with_needs(attention("moba", "mv"), [("evac", mv[1]["g"])])
        conv = lambda t: [side("conv", tile=t, layer=l, needs=[("evac", cg[1]["g"]), ("unit", va[1]["g"])])]
        sides += moba
        sides += [norm("qn", 4, f"{pre}_qn_g", "qn", 1.0 / 64, mat="blk64", needs=[("evac", va[1]["g"])])]
        sides += [norm("kn", 4, f"{pre}_kn_g", "kn", 1.0 / 64, mat="blk64")]
        sides += [norm("qp", 2, f"{pre}_qr_g", "qp", 1.0 / 32, mat="blk32", post=("rope", "32"))]
        sides += attention("mla", "va")
        for t in range(4):
            sides += conv(t)
        sides += [side("center", needs=[])]
        sides += [norm("ca", 4, f"{pre}_ln_g", "ca", 1.0 / 512, total=True, post=("silu", f"{pre}_ln_b"))]
        units = lat + mq + mk + mv + uq + kn + va + ca + cg + gates
        items = units[:3] + [sides[0], sides[1]] + merge(units[3:], sides[2:], lead=4)
        if l == 0:
            items = spread(items, adas(2, 24, 24), 1)
        plan.extend(items)
        plan.append(fence())
        items = f_units("w_mla", (l,), 4, 1024, "qn", [evac("gate", "g0", u, 0) for u in range(4)])
        items += f_units("w_moba", (l,), 4, 1024, "mq", [evac("gate", "g1", u, 1) for u in range(4)])
        items += f_units("w_pw", (l,), 4, 1024, "ca", [evac("gate_bias", "g2", u, f"{pre}_pw_b") for u in range(4)])
        plan.extend(items)
        plan.append(fence())
        for i in range(2):
            plan.extend(f_units("w_o2", (l, i), DK, 512, "h", [evac("resid", L, 16, 2 * i + u) for u in range(2)]))
        plan.append(fence())
        plan.extend(modulate(L, pre, "ffn_g", 24, 32))
        plan.append(fence())
        items = glu_units("up", (l,), FF_U, lambda i: (evac("fir_a", l, i), evac("fir_b", l, i)))
        if l == 0:
            items = spread(items, adas(3, 0, 24), 1)
        plan.extend(items)
        plan.append(fence())
        plan.extend(down_units("down", (l,), 22, "hid", lambda i: evac("resid", L, 40, i)))
        plan.append(fence())
    plan.append(dict(kind="end"))
    return plan


class Book:

    def __init__(self):
        self.known, self.whole = {}, {}
        self.restart()

    def restart(self):
        self.at, self.count = {}, {}


class Count:

    def __init__(self, name, book):
        self.name, self.book = name, book

    def step(self, *keys, of=None, by=1):
        name = of or self.name
        self.book.count[name] = self.book.count.get(name, 0) + by
        for key in keys:
            self.mark(*key, of=name)
        return by

    def mark(self, *key, of=None):
        name = of or self.name
        self.book.at[key] = (name, self.book.count.get(name, 0))

    def at(self, *key):
        return self.book.known[key][1] if key in self.book.known else 0

    def by(self, *key):
        return self.book.known.get(key, (self.name,))[0]

    def now(self):
        return self.book.count.get(self.name, 0)


class Rounds(Count):

    def __init__(self, name, book, n):
        self.name, self.book, self.n = "round_" + name, book, n

    def share(self, name=None):
        return self.book.whole.get("round_" + name if name else self.name, 1)

    def at(self, *key, last_round=False):
        name, count = self.book.known.get(key, (self.name, 1))
        per = self.book.whole.get(name, 1)
        if last_round or name.startswith("round_slot"):
            return self.n * per + count
        return self.n * per + count + per

    def now(self):
        return self.n * self.share() + self.share() + self.book.count.get(self.name, 0)


def build(nc, arrays, out, book, ccols, ccons):
    colat, ncol = column_map()
    conat, ncon = constant_map()
    plan = make_plan()
    with ExitStack() as ctx:
        def sb(name, shape, dt=F32):
            return ctx.enter_context(nc.sbuf_tensor(name, shape, dt))

        xT = sb("xT", [P, 8, T])
        hT = sb("hT", [P, 8, T])
        ring = sb("ring", [P, RING, SLOT])
        mod_in = sb("mod_in", [P, 2, MODW])
        mod_acc = sb("mod_acc", [P, ACCS, 256])
        ada = sb("ada", [P, 2, 48])
        act_c = sb("act_c", [P, 2, 8])
        acol = sb("acol", [P, 8])
        cols = sb("cols", [P, ncol])
        cons = sb("cons", [P, ncon])
        small = sb("small", [P, 160])
        WN = 22144
        pos = sb("pos", [P, T], I32)
        work = sb("work", [P, WN])
        psum = ctx.enter_context(nc.psum_tensor("psum", [P, 8, 512], F32))

        def region(off, nt, w=T):
            return work[:, off:off + nt * w].rearrange("p (a b) -> p a b", b=w)

        R = {"x": xT[:, :, :], "h": hT[:, :, :]}
        off = 0
        for name, nt in (("q", 4), ("z", 4), ("hg", 4), ("dq", 4), ("dk", 4), ("ga", 8), ("gb", 8)):
            R[name] = region(off, nt)
            off += nt * T
        for name in ("v", "dv"):
            R[name] = region(off, 2, 512)
            off += 1024
        hb = off
        for name in ("b", "e", "qt", "kt", "kin"):
            R[name] = region(off, 4)
            off += 1024
        R["sc"] = region(off, 3, 512)
        off += 1536
        assert off <= WN
        off = 0
        R["lat"] = region(off, 6)
        R["ql"], R["kl"], R["kr"] = region(off, 3), region(off + 3 * T, 2), region(off + 5 * T, 1)
        R["ca"] = region(off, 4)
        off += 6 * T
        for name, nt in (("mq", 4), ("mk", 4), ("gates", 24), ("qn", 4), ("kn", 4), ("qp", 2)):
            R[name] = region(off, nt)
            off += nt * T
        R["g0"], R["g1"], R["g2"] = R["gates"][:, 0:8, :], R["gates"][:, 8:16, :], R["gates"][:, 16:24, :]
        for name in ("mv", "va"):
            R[name] = region(off, 2, 512)
            off += 1024
        PADT = T + CONV_W - 1
        R["cu"] = region(off, 4, PADT)
        off += 4 * PADT
        R["cos64"], R["sin64"], R["cos32"], R["sin32"] = (region(off + i * T, 1) for i in range(4))
        off += 4 * T
        temp2 = off
        assert temp2 + 4096 + 1536 <= WN, temp2
        R["hid"] = region(0, 28)
        R["silu"] = region(36 * T, 4)
        off = 0
        h_tok = region(off, 2, D)
        off += 2 * D
        pick, weigh = region(off, 2, P), region(off + T, 2, P)
        off += 2 * T
        picked = region(off, DK, P)
        off += D
        back = work[:, off:off + T]
        off += T
        up_s, hid_s = region(off, 2), region(off + 2 * T, 2)
        off += 4 * T
        hid_e = region(off, D_FE // P, P)
        off += D_FE
        y_e = work[:, off:off + D]
        off += D
        assert off <= hb
        route = small[:, 112:144]
        now4 = small[:, 144:148]
        passes = sb("passes", [P, 1], I32)
        R["fir"] = region(44 * T, 8)
        assert 52 * T <= temp2 - 1024
        R["conv_gate"] = R["gates"][:, 22:24, :]

        def temps(s_item):
            base = temp2 if s_item.get("block2") else hb
            sq = region(base, 8)
            return sq, region(base + 2048, 4), region(base + 3072, 4), region(base, 4)

        def soft(s_item):
            base = (temp2 + 4096) if s_item.get("block2") else hb + 4096
            return (work[:, base:base + 512].rearrange("p (c n) -> p c n", c=2),
                    work[:, base + 512:base + 1024].rearrange("p (c n) -> p c n", c=2),
                    work[:, base + 1024:base + 1536])

        block2 = False
        for it in plan:
            if it["kind"] == "rope_tables":
                block2 = True
            it["block2"] = block2

        def col(name, i=0, n=1):
            o, w = colat[name]
            assert i + n <= w
            return cols[:, o + i:o + i + n]

        def con(name, i=0, n=None):
            o, w = conat[name]
            return cons[:, o + i:o + (i + n if n else w)]

        def gbank(b):
            return psum[:, b, :].rearrange("p (a t) -> p a t", t=T)

        def sbank(i):
            return psum[:, GBANKS + i, :]

        ada_bank = psum[:, 7, :]

        def sem(name):
            return ctx.enter_context(nc.semaphore(name))

        tensor_done, scalar_done = sem("tensor_done"), sem("scalar_done")
        vector_done, gpsimd_done = sem("vector_done"), sem("gpsimd_done")
        inputs_loaded, stored = sem("inputs_loaded"), sem("stored")
        slot_loaded = [sem(f"slot{i}_loaded") for i in range(RING)]
        mod_loaded = [sem(f"mod{i}_loaded") for i in range(2)]
        done = {"PE": tensor_done, "ACT": scalar_done, "DVE": vector_done, "POOL": gpsimd_done}
        book.restart()
        vector_pass = sem("vector_pass")
        tensor_round, scalar_round, vector_round = sem("tensor_round"), sem("scalar_round"), sem("vector_round")
        rounds = {"round_PE": tensor_round, "round_ACT": scalar_round, "round_DVE": vector_round}
        round_loaded = [sem(f"round_slot{i}_loaded") for i in range(RING)]
        cut = [i for i, it in enumerate(plan) if it["kind"] == "experts"]
        before, after = (plan[:cut[0]], plan[cut[0] + 1:]) if cut else (plan, [])

        block = ctx.enter_context(nc.Block())

        @block.sync
        def _(sp):
            w = Count("SP", book)
            used, fences = {}, []
            sp.dma_start(cols[:, :], ccols).then_inc(inputs_loaded, w.step(of="inputs", by=16))
            sp.dma_start(cons[:, :], ccons).then_inc(inputs_loaded, w.step(of="inputs", by=16))
            sp.dma_start(xT[:, :, :], arrays["xT"]).then_inc(inputs_loaded, w.step(of="inputs", by=16))
            sp.dma_start(pos[:, :], arrays["positions"].to_broadcast([P, T])).then_inc(
                inputs_loaded, w.step(("inputs",), of="inputs", by=16))

            def run(steps):
                for it in steps:
                    if it["kind"] == "fence":
                        fences.append(it["n"])
                    for c in it["load"] if it["kind"] == "unit" else ():
                        last = used.get(c["slot"])
                        if last is not None:
                            sp.wait_ge(tensor_done, w.at("used", last["n"]))
                        used[c["slot"]] = c
                        src = arrays[c["name"]]
                        for i in c["idx"]:
                            src = src[i]
                        sp.dma_start(ring[:, c["slot"], 0:c["width"]], src).then_inc(
                            slot_loaded[c["slot"]], w.step(("loaded", c["n"]), of=f"slot{c['slot']}", by=16))

            run(before)
            if after:
                for c in used.values():
                    sp.wait_ge(tensor_done, w.at("used", c["n"]))
                sp.wait_ge(vector_done, w.at("passes"))
                n_passes = sp.value_load(passes[0:1, 0:1], min_val=1, max_val=2)
                with sp.Fori(0, n_passes) as p:
                    with sp.Fori(0, EXPERTS) as e:
                        r = Rounds("SP", book, p * EXPERTS + e)
                        for c in range(EXPERT_CHUNKS):
                            slot = c % RING
                            src = arrays["m13"][e, c] if c < FE_U else arrays["m2"][e, (c - FE_U) // 4, (c - FE_U) % 4]
                            n = SLOT if c < FE_U else 7 * 512
                            if c >= RING:
                                sp.wait_ge(tensor_round, r.at("r_used", c - RING))
                            else:
                                last = EXPERT_CHUNKS - 1 - (EXPERT_CHUNKS - 1 - c) % RING
                                sp.wait_ge(tensor_round, r.at("r_used", last, last_round=True))
                            sp.dma_start(ring[:, slot, 0:n], src).then_inc(
                                round_loaded[slot], r.step(("r_loaded", c), of=f"round_slot{slot}", by=16))
                sp.wait_ge(tensor_done, w.at("experts_over", "PE"))
                used.clear()
            run(after)
            sp.wait_ge(vector_done, w.at("fence", fences[-1], "DVE"))
            sp.dma_start(out, xT[:, :, :]).then_inc(stored, 16)
            sp.wait_ge(stored, 16)

        @block.tensor
        def _(pe):
            w = Count("PE", book)

            def begin(it):
                if it["s"]:
                    pe.wait_ge(tensor_done, w.at("side", it["s"] - 1, "PE"))
                    pe.wait_ge(scalar_done, w.at("side", it["s"] - 1, "ACT"))
                    pe.wait_ge(vector_done, w.at("side", it["s"] - 1, "DVE"))
                for key in it["needs"]:
                    pe.wait_ge(done[w.by(*key)], w.at(*key))

            def fence(it):
                w.mark("fence", it["n"], "PE")
                pe.wait_ge(scalar_done, w.at("fence", it["n"], "ACT"))
                pe.wait_ge(vector_done, w.at("fence", it["n"], "DVE"))

            mm, ev = nc.tensor.matmul, {}

            def unit(it):
                g = it["g"]
                prev = ev.get(it["bank"])
                if prev is not None:
                    pe.wait_ge(done[w.by("evac", prev)], w.at("evac", prev))
                ev[it["bank"]] = g
                for key in it["ready"]:
                    if key[0] == "side_done":
                        pe.wait_ge(vector_done, w.at("side", key[1], "DVE"))
                    else:
                        pe.wait_ge(done[w.by(*key)], w.at(*key))
                rhs = R[it["rhs"]]
                total = sum(p[1] for p in it["parts"])
                n = 0
                if it["mode"] == "F":
                    for j in range(2):
                        n = 0
                        for c, kt, width, col0, k0 in it["parts"]:
                            pe.wait_ge(slot_loaded[c["slot"]], w.at("loaded", c["n"]))
                            wt = ring[:, c["slot"], 0:kt * width].rearrange("p (k n) -> p k n", n=width)
                            for k in range(kt):
                                last = mm(gbank(it["bank"])[:, j, :], wt[:, k, col0 + j * P:col0 + (j + 1) * P],
                                          rhs[:, k0 + k, :], start=(n == 0), stop=(n == total - 1))
                                n += 1
                else:
                    (c, kt, width, col0, k0), = it["parts"]
                    pe.wait_ge(slot_loaded[c["slot"]], w.at("loaded", c["n"]))
                    wt = ring[:, c["slot"], 0:kt * width].rearrange("p (k n) -> p k n", n=width)
                    for k in range(kt):
                        last = mm(psum[:, it["bank"], :], rhs[:, k, it["tile"] * P:(it["tile"] + 1) * P],
                                  wt[:, k, col0:col0 + 512], start=(k == 0), stop=(k == kt - 1))
                last.then_inc(tensor_done, w.step(("unit", g), *[("used", c["n"]) for c in it["free"]]))

            def ada_step(it):
                n = it["n"]
                pe.wait_ge(gpsimd_done, w.at("mod_acc", n))
                if n:
                    pe.wait_ge(vector_done, w.at("ada", n - 1))
                for j in range(2):
                    last = mm(ada_bank[:, j:j + 1], mod_acc[:, n % ACCS, j * P:(j + 1) * P], con("ones", 0, 1),
                              start=True, stop=True)
                last.then_inc(tensor_done, w.step(("ada_sum", n)))

            def norm(it):
                begin(it)
                sq = temps(it)[0]
                pe.wait_ge(scalar_done, w.at("squares", it["s"]))
                nt = it["nt"]
                for t in range(nt):
                    if it["total"]:
                        last = mm(sbank(0)[:, 0:T], con(it["mat"], 0, P), sq[:, t, :], start=(t == 0), stop=(t == nt - 1))
                    else:
                        last = mm(sbank(t // 2)[:, (t % 2) * T:(t % 2 + 1) * T], con(it["mat"], 0, P), sq[:, t, :],
                                  start=True, stop=True)
                last.then_inc(tensor_done, w.step(("sums", it["s"])))
                if it["post"] and it["post"][0] == "rope":
                    pe.wait_ge(vector_done, w.at("scaled", it["s"]))
                    for t in range(nt):
                        last = mm(sbank(2 + t // 2)[:, (t % 2) * T:(t % 2 + 1) * T], con("rot" + it["post"][1]),
                                  R[it["dst"]][:, t, :], start=True, stop=True)
                    last.then_inc(tensor_done, w.step(("turned", it["s"])))

            def hg_level(it):
                begin(it)
                n = it["level"]
                k, q = (R["kin"], R["q"]) if n == 0 else (R["kt"], R["qt"])
                pe.wait_ge(vector_done, w.at("decayed", it["s"]))
                if n == 128:
                    for h in range(4):
                        last = mm(sbank(0)[:, h * P:(h + 1) * P], k[:, h, 0:P], q[:, h, P:T], start=True, stop=True)
                else:
                    for t in range(2):
                        for h in range(4):
                            last = mm(sbank(t)[:, h * P:(h + 1) * P], k[:, h, t * P:(t + 1) * P],
                                      q[:, h, t * P:(t + 1) * P], start=True, stop=True)
                last.then_inc(tensor_done, w.step(("level", it["s"])))

            def hg_out(it):
                begin(it)
                v, sc = R["v"], R["sc"]
                for h in range(4):
                    o = sbank(2 + h // 2)[:, (h % 2) * T:(h % 2 + 1) * T]
                    cut = slice(h * P, (h + 1) * P)
                    mm(o[:, 0:P], v[:, 0, cut], sc[:, 0, cut], start=True, stop=True)
                    mm(o[:, P:T], v[:, 0, cut], sc[:, 1, cut], start=True, stop=False)
                    last = mm(o[:, P:T], v[:, 1, cut], sc[:, 2, cut], start=False, stop=True)
                last.then_inc(tensor_done, w.step(("hg_o", it["s"])))

            def attn(it):
                begin(it)
                soft_s, soft_w, turned = soft(it)
                what = it["what"]
                if it["out"]:
                    i, q = it["out"]
                    v = R[it["v"]]
                    for c in range(1 if what == "diff" else 2):
                        for kt in range(q + 1):
                            last = mm(sbank(3)[:, c * P:(c + 1) * P], v[:, kt, i * P:(i + 1) * P],
                                      turned[:, (c * 2 + kt) * P:(c * 2 + kt + 1) * P], start=(kt == 0), stop=(kt == q))
                    last.then_inc(tensor_done, w.step(("attn_out", it["s"])))
                if it["turn"]:
                    i, q = it["turn"]
                    for c in range(1 if what == "diff" else 2):
                        for kt in range(q + 1):
                            last = nc.tensor.transpose(sbank(2)[:, (c * 2 + kt) * P:(c * 2 + kt + 1) * P],
                                                       soft_w[:, c, kt * P:(kt + 1) * P], con("ident"))
                    last.then_inc(tensor_done, w.step(("attn_turn", it["s"])))
                if it["load"]:
                    i, q = it["load"]
                    n = (q + 1) * P
                    for c in range(2):
                        o = sbank(c)[:, 0:n]
                        rows = slice(c * 64, c * 64 + 64)
                        Q, K = {"diff": ("dq", "dk"), "moba": ("mq", "mk"), "mla": ("qn", "kn")}[what]
                        last = mm(o, R[Q][rows, i, q * P:(q + 1) * P], R[K][rows, i, 0:n], start=True,
                                  stop=(what != "mla"))
                        if what == "mla":
                            last.then_inc(tensor_done, w.step())
                            pe.wait_ge(tensor_done, w.now())
                            h = 2 * i + c
                            rows = slice((h % 4) * 32, (h % 4) * 32 + 32)
                            last = mm(o, R["qp"][rows, h // 4, q * P:(q + 1) * P], R["kr"][rows, 0, 0:n],
                                      start=False, stop=True)
                    last.then_inc(tensor_done, w.step(("scores", it["s"])))

            def expert(r, e):
                def bank(b):
                    if b >= GBANKS:
                        k = ("r_evac", b - GBANKS)
                        pe.wait_ge(rounds[r.book.known.get(k, ("round_PE",))[0]], r.at(*k))
                    else:
                        k = ("r_evac", ROUND_BANKS - 1 - (ROUND_BANKS - 1 - b) % GBANKS)
                        pe.wait_ge(vector_round, r.at(*k, last_round=True))
                    return psum[:, b % GBANKS, :]

                pe.wait_ge(vector_round, r.at("r_pick"))
                for half in range(2):
                    o = bank(half)
                    for f in range(4):
                        for t in range(2):
                            last = mm(o[:, f * P:(f + 1) * P], h_tok[:, t, (4 * half + f) * P:(4 * half + f + 1) * P],
                                      pick[:, t, :], start=(t == 0), stop=(t == 1))
                    last.then_inc(tensor_round, r.step(("r_bank", half)))
                pe.wait_ge(vector_round, r.at("r_weigh"))
                pe.wait_ge(scalar_round, r.at("r_turned", FE_U - 1, last_round=True))
                for t in range(2):
                    last = nc.tensor.transpose(sbank(2)[:, t * P:(t + 1) * P], weigh[:, t, :], con("ident"))
                last.then_inc(tensor_round, r.step(("r_weights",)))
                pe.wait_ge(scalar_round, r.at("r_picked"))

                def turn(i):
                    pe.wait_ge(vector_round, r.at("r_evac", 2 + i))
                    if i >= 2:
                        pe.wait_ge(scalar_round, r.at("r_turned", i - 2))
                    for j in range(2):
                        last = nc.tensor.transpose(sbank(i % 2)[:, j * P:(j + 1) * P],
                                                   hid_s[:, i % 2, j * P:(j + 1) * P], con("ident"))
                    last.then_inc(tensor_round, r.step(("r_turn", i)))

                for i in range(FE_U):
                    o = bank(2 + i)
                    pe.wait_ge(round_loaded[i % RING], r.at("r_loaded", i))
                    wt = ring[:, i % RING, :].rearrange("p (k n) -> p k n", n=512)
                    for k in range(DK):
                        last = mm(o, picked[:, k, :], wt[:, k, :], start=(k == 0), stop=(k == DK - 1))
                    last.then_inc(tensor_round, r.step(("r_bank", 2 + i), ("r_used", i)))
                    if i:
                        turn(i - 1)
                turn(FE_U - 1)
                for half in range(2):
                    o = bank(2 + FE_U + half)
                    for kg in range(4):
                        c = FE_U + 4 * half + kg
                        pe.wait_ge(round_loaded[c % RING], r.at("r_loaded", c))
                        wt = ring[:, c % RING, 0:7 * 512].rearrange("p (k n) -> p k n", n=512)
                        for k in range(7):
                            if half == 0 and kg == 3 and k == 5:
                                pe.wait_ge(scalar_round, r.at("r_turned", FE_U - 1))
                            elif half == 0 and k == 0:
                                pe.wait_ge(scalar_round, r.at("r_turned", min(FE_U - 2, (7 * kg + 6) // 2)))
                            last = mm(o, hid_e[:, 7 * kg + k, :], wt[:, k, :], start=(kg == 0 and k == 0),
                                      stop=(kg == 3 and k == 6))
                        last.then_inc(tensor_round, r.step(("r_bank", 2 + FE_U + half), ("r_used", c)))
                pe.wait_ge(vector_round, r.at("r_back"))
                for u in range(4):
                    o = bank(4 + FE_U + u)
                    pe.wait_ge(scalar_round, r.at("r_evac", 2 + FE_U + u // 2))
                    for j in range(2):
                        last = mm(o[:, j * T:(j + 1) * T], y_e[:, (2 * u + j) * P:(2 * u + j + 1) * P], back,
                                  start=True, stop=True)
                    last.then_inc(tensor_round, r.step(("r_bank", 4 + FE_U + u)))

            def run(steps):
                for it in steps:
                    kind = it["kind"]
                    if kind == "unit":
                        unit(it)
                    elif kind == "ada":
                        ada_step(it)
                    elif kind == "fence":
                        fence(it)
                    elif kind == "end":
                        pass
                    else:
                        if kind == "norm":
                            norm(it)
                        elif kind == "hg_level":
                            hg_level(it)
                        elif kind == "hg_out":
                            hg_out(it)
                        elif kind == "attn":
                            attn(it)
                        elif kind == "lam":
                            begin(it)
                            pe.wait_ge(vector_done, w.at("lam_products", it["s"]))
                            mm(sbank(0)[:, 0:2], con("blk64"), small[:, 0:2], start=True, stop=True).then_inc(tensor_done, w.step(("lam_sums", it["s"])))
                        elif kind == "center":
                            begin(it)
                            for t in range(4):
                                last = mm(sbank(0)[:, 0:T], con("ones", 0, P), R["ca"][:, t, :], start=(t == 0), stop=(t == 3))
                            last.then_inc(tensor_done, w.step(("center", it["s"])))
                        elif kind == "router":
                            begin(it)
                            for t in range(2):
                                for k in range(DK):
                                    last = mm(sbank(0)[:, t * 8:t * 8 + 8], R["h"][:, k, t * P:(t + 1) * P],
                                              col("router", 8 * k, 8), start=(k == 0), stop=(k == DK - 1))
                            last.then_inc(tensor_done, w.step(("logits", it["s"])))
                            pe.wait_ge(vector_done, w.at("chosen", it["s"]))
                            sel = small[:, 88:104]
                            o = sbank(0)
                            mm(o[:, 16:24], con("earlier"), sel[:, 0:8], start=True, stop=True)
                            mm(o[:, 24:32], con("ones", 0, P), sel[:, 0:8], start=True, stop=False)
                            mm(o[:, 24:32], con("earlier"), sel[:, 8:16], start=False, stop=True)
                            for t in range(2):
                                last = mm(o[:, 32:40], con("ones", 0, P), sel[:, 8 * t:8 * t + 8], start=(t == 0),
                                          stop=(t == 1))
                            last.then_inc(tensor_done, w.step(("places", it["s"])))
                            for half in range(4):
                                t, q = half // 2, half % 2
                                if half == 3:
                                    pe.wait_ge(vector_done, w.at("placed", it["s"]))
                                for f in range(4):
                                    last = nc.tensor.transpose(sbank((half + 1) % 4)[:, f * P:(f + 1) * P],
                                                               R["h"][:, 4 * q + f, t * P:(t + 1) * P], con("ident"))
                            last.then_inc(tensor_done, w.step(("h_turned", it["s"])))
                        w.mark("side", it["s"], w.name)

            run(before)
            if after:
                pe.wait_ge(vector_done, w.at("passes"))
                n_passes = pe.value_load(passes[0:1, 0:1], min_val=1, max_val=2)
                pe.drain().then_inc(tensor_round, Rounds("PE", book, 0).share())
                with pe.Fori(0, n_passes) as p:
                    with pe.Fori(0, EXPERTS) as e:
                        expert(Rounds("PE", book, p * EXPERTS + e), e)
                pe.drain().then_inc(tensor_done, w.step(("experts_over", "PE")))
            run(after)

        @block.scalar
        def _(act):
            w = Count("ACT", book)

            def begin(it):
                if it["s"]:
                    act.wait_ge(scalar_done, w.at("side", it["s"] - 1, "ACT"))
                    act.wait_ge(tensor_done, w.at("side", it["s"] - 1, "PE"))
                    act.wait_ge(vector_done, w.at("side", it["s"] - 1, "DVE"))
                for key in it["needs"]:
                    act.wait_ge(done[w.by(*key)], w.at(*key))

            def fence(it):
                w.mark("fence", it["n"], "ACT")
                act.wait_ge(tensor_done, w.at("fence", it["n"], "PE"))
                act.wait_ge(vector_done, w.at("fence", it["n"], "DVE"))

            A = nc.scalar.activation

            def unit(it):
                e, g = it["evac"], it["g"]
                if e[0] == "act":
                    act.wait_ge(tensor_done, w.at("unit", g))
                    for key in it["after"]:
                        act.wait_ge(vector_done, w.at(*key))
                    if it["mode"] == "F":
                        dst, src = R[e[2]][:, 2 * e[3]:2 * e[3] + 2, :], gbank(it["bank"])
                    else:
                        dst, src = R[e[2]][:, e[3], :], psum[:, it["bank"], :]
                    A(dst, src, {"Copy": ACT.Copy, "Silu": ACT.Silu, "Sigmoid": ACT.Sigmoid}[e[1]]).then_inc(scalar_done, w.step(("evac", g)))
                elif e[0] == "conv_in":
                    act.wait_ge(tensor_done, w.at("unit", g))
                    u = e[2]
                    if e[1] == "Copy":
                        A(R["cu"][:, 2 * u:2 * u + 2, CONV_W - 1:PADT], gbank(it["bank"]), ACT.Copy).then_inc(scalar_done, w.step(("evac", g)))
                    else:
                        act.wait_ge(vector_done, w.at("conv_gate_used", it["g"] - 1))
                        A(R["conv_gate"], gbank(it["bank"]), ACT.Sigmoid).then_inc(scalar_done, w.step(("evac", g)))
                elif e[0] == "glu_a":
                    act.wait_ge(tensor_done, w.at("unit", g))
                    if e[1] >= 2:
                        act.wait_ge(vector_done, w.at("evac", g - 3))
                    A(R["silu"][:, 2 * (e[1] % 2):2 * (e[1] % 2) + 2, :], gbank(it["bank"]), ACT.Silu).then_inc(scalar_done, w.step(("glu_a", g)))
                    w.mark("evac", g)
                elif e[0] in ("fir_a", "fir_b"):
                    act.wait_ge(tensor_done, w.at("unit", g))
                    l, i = e[1], e[2]
                    act.wait_ge(vector_done, w.at("fir_used", g - 2))
                    b = 4 * (i % 2) + (2 if e[0] == "fir_b" else 0)
                    for j in range(2):
                        tile = (0 if e[0] == "fir_a" else 22) + 2 * i + j
                        A(R["fir"][:, b + j, :], gbank(it["bank"])[:, j, :], ACT.Identity,
                                 bias=col(f"b{l}_fb", tile), scale=col(f"b{l}_fw", 2 * 44 + tile)).then_inc(scalar_done, w.step(("fir_0", g)))
                    if e[0] == "fir_b":
                        a = 4 * (i % 2)
                        act.wait_ge(vector_done, w.at("fir_sum", g - 1))
                        act.wait_ge(scalar_done, w.now())
                        A(R["fir"][:, a:a + 2, :], R["fir"][:, a:a + 2, :], ACT.Silu).then_inc(scalar_done, w.step(("fir_silu", g)))

            def norm(it):
                begin(it)
                sq, t1, y, _ = temps(it)
                nt = it["nt"]
                src = R[it["src"]]
                n = T if it["total"] else nt * T
                A(sq[:, 0:nt, :], src[:, 0:nt, :], ACT.Square).then_inc(scalar_done, w.step(("squares", it["s"])))
                act.wait_ge(vector_done, w.at("mean", it["s"]))
                nn = 1 if it["total"] else nt
                A(y[:, 0:nn, :], t1[:, 0:nn, :], ACT.Ln).then_inc(scalar_done, w.step())
                act.wait_ge(scalar_done, w.now())
                A(y[:, 0:nn, :], y[:, 0:nn, :], ACT.Exp, scale=-0.5).then_inc(scalar_done, w.step(("root", it["s"])))
                post = it["post"]
                if post and post[0] == "shift":
                    for t in range(nt):
                        act.wait_ge(vector_done, w.at("scaled_tile", it["s"], t))
                        A(R["h"][:, t, :], R["h"][:, t, :], ACT.Identity,
                                 bias=ada[:, post[1] % 2, post[2] + t:post[2] + t + 1]).then_inc(scalar_done, w.step())
                if post and post[0] == "silu":
                    for t in range(nt):
                        act.wait_ge(vector_done, w.at("scaled_tile", it["s"], t))
                        A(R[it["dst"]][:, t, :], R[it["dst"]][:, t, :], ACT.Silu, bias=col(post[1], t)).then_inc(scalar_done, w.step())

            def hg_prep(it):
                begin(it)
                A(R["kin"], R["z"], ACT.Sigmoid, scale=-1.0).then_inc(scalar_done, w.step(("kin", it["s"])))
                if it["layer"] == 0:
                    act.wait_ge(vector_done, w.at("abs_z", it["s"]))
                    A(R["e"], R["e"], ACT.Exp, scale=-1.0).then_inc(scalar_done, w.step())
                    act.wait_ge(scalar_done, w.now())
                    A(R["e"], R["e"], ACT.Ln, bias=1.0).then_inc(scalar_done, w.step(("softplus", it["s"])))
                else:
                    A(R["e"], R["z"], ACT.Sigmoid).then_inc(scalar_done, w.step())
                    act.wait_ge(vector_done, w.at("lb_in", it["s"]))
                    A(small[:, 8:12], small[:, 8:12], ACT.Sigmoid).then_inc(scalar_done, w.step(("lb", it["s"])))
                    act.wait_ge(vector_done, w.at("forget", it["s"]))
                    A(R["qt"], R["e"], ACT.Ln).then_inc(scalar_done, w.step(("log_f", it["s"])))

            def attn(it):
                begin(it)
                soft_s, soft_w, turned = soft(it)
                what = it["what"]
                if it["turn"]:
                    i, q = it["turn"]
                    act.wait_ge(tensor_done, w.at("attn_turn", it["s"]))
                    act.wait_ge(tensor_done, w.at("attn_out", it["s"]))
                    for c in range(1 if what == "diff" else 2):
                        n = (q + 1) * P
                        last = A(turned[:, c * 256:c * 256 + n], sbank(2)[:, c * 256:c * 256 + n], ACT.Copy)
                        last.then_inc(scalar_done, w.step())
                if it["load"]:
                    i, q = it["load"]
                    n = (q + 1) * P
                    act.wait_ge(vector_done, w.at("neg_max", it["s"]))
                    for c in range(2):
                        A(soft_s[:, c, 0:n], soft_s[:, c, 0:n], ACT.Exp, bias=small[:, 22 + c:23 + c],
                                 accum_out=small[:, 24 + c:25 + c]).then_inc(scalar_done, w.step(("exps", it["s"])))

            def expert(r, e):
                for half in range(2):
                    act.wait_ge(tensor_round, r.at("r_bank", half))
                    act.wait_ge(tensor_round, r.at("r_used", FE_U - 1, last_round=True))
                    A(picked[:, 4 * half:4 * half + 4, :], psum[:, half, :].rearrange("p (f n) -> p f n", n=P),
                      ACT.Copy).then_inc(scalar_round, r.step(("r_evac", half), ("r_picked",)))

                def turned(i):
                    act.wait_ge(tensor_round, r.at("r_turn", i))
                    if i == 0:
                        act.wait_ge(tensor_round, r.at("r_used", EXPERT_CHUNKS - 1, last_round=True))
                    A(hid_e[:, 2 * i:2 * i + 2, :], sbank(i % 2)[:, 0:T].rearrange("p (j n) -> p j n", n=P),
                      ACT.Copy).then_inc(scalar_round, r.step(("r_turned", i)))

                for i in range(FE_U):
                    act.wait_ge(tensor_round, r.at("r_bank", 2 + i))
                    if i >= 2:
                        act.wait_ge(vector_round, r.at("r_evac", i))
                    A(up_s[:, i % 2, :], psum[:, (2 + i) % GBANKS, 0:T], ACT.Silu).then_inc(
                        scalar_round, r.step(("r_silu", i)))
                    if i:
                        turned(i - 1)
                turned(FE_U - 1)
                for half in range(2):
                    act.wait_ge(tensor_round, r.at("r_bank", 2 + FE_U + half))
                    act.wait_ge(tensor_round, r.at("r_bank", ROUND_BANKS - 1, last_round=True))
                    A(y_e[:, half * 512:(half + 1) * 512], psum[:, (2 + FE_U + half) % GBANKS, :],
                      ACT.Copy).then_inc(scalar_round, r.step(("r_evac", 2 + FE_U + half)))

            def run(steps):
                for it in steps:
                    kind = it["kind"]
                    if kind == "unit":
                        unit(it)
                    elif kind == "fence":
                        fence(it)
                    elif kind in ("ada", "end"):
                        pass
                    else:
                        if kind == "norm":
                            norm(it)
                        elif kind == "start":
                            act.wait_ge(inputs_loaded, w.at("inputs"))
                            A(act_c[:, 0, :], col("c1", 0, 8), ACT.Silu).then_inc(scalar_done, w.step())
                            A(act_c[:, 1, :], col("c2", 0, 8), ACT.Silu).then_inc(scalar_done, w.step(("silu_c",)))
                        elif kind == "hg_prep":
                            hg_prep(it)
                        elif kind == "hg_level" and it["level"] > 0:
                            begin(it)
                            act.wait_ge(vector_done, w.at("spans", it["s"]))
                            A(R["e"], R["e"], ACT.Exp).then_inc(scalar_done, w.step(("decays", it["s"])))
                        elif kind == "hg_out":
                            begin(it)
                            act.wait_ge(tensor_done, w.at("hg_o", it["s"]))
                            for i in range(2):
                                A(R["z"][:, 2 * i:2 * i + 2, :], sbank(2 + i).rearrange("p (a t) -> p a t", t=T),
                                         ACT.Copy).then_inc(scalar_done, w.step())
                        elif kind == "attn":
                            attn(it)
                        elif kind == "lam":
                            begin(it)
                            act.wait_ge(tensor_done, w.at("lam_sums", it["s"]))
                            A(small[:, 2:4], sbank(0)[:, 0:2], ACT.Exp).then_inc(scalar_done, w.step(("lam_exps", it["s"])))
                        elif kind == "router":
                            begin(it)
                            act.wait_ge(vector_done, w.at("neg_max", it["s"]))
                            for t in range(2):
                                A(small[:, 64 + 8 * t:72 + 8 * t], small[:, 48 + 8 * t:56 + 8 * t], ACT.Exp,
                                         bias=small[:, 82 + t:83 + t]).then_inc(scalar_done, w.step(("exps", it["s"])))
                        elif kind == "rope_tables":
                            begin(it)
                            for j, name in enumerate(("64", "32")):
                                act.wait_ge(vector_done, w.at("angle", it["s"], j))
                                A(R["sin" + name], R["cos" + name], ACT.Sin).then_inc(scalar_done, w.step(("sin", it["s"], j)))
                                A(R["cos" + name], R["cos" + name], ACT.Sin, scale=0.5).then_inc(scalar_done, w.step(("half", it["s"], j)))
                        w.mark("side", it["s"], w.name)

            run(before)
            if after:
                act.wait_ge(vector_done, w.at("passes"))
                n_passes = act.value_load(passes[0:1, 0:1], min_val=1, max_val=2)
                act.drain().then_inc(scalar_round, Rounds("ACT", book, 0).share())
                with act.Fori(0, n_passes) as p:
                    with act.Fori(0, EXPERTS) as e:
                        expert(Rounds("ACT", book, p * EXPERTS + e), e)
                act.drain().then_inc(scalar_done, w.step(("experts_over", "ACT")))
            run(after)

        @block.vector
        def _(dve):
            w = Count("DVE", book)

            def begin(it):
                if it["s"]:
                    dve.wait_ge(vector_done, w.at("side", it["s"] - 1, "DVE"))
                    dve.wait_ge(tensor_done, w.at("side", it["s"] - 1, "PE"))
                    dve.wait_ge(scalar_done, w.at("side", it["s"] - 1, "ACT"))
                for key in it["needs"]:
                    dve.wait_ge(done[w.by(*key)], w.at(*key))

            def fence(it):
                w.mark("fence", it["n"], "DVE")
                dve.wait_ge(tensor_done, w.at("fence", it["n"], "PE"))
                dve.wait_ge(scalar_done, w.at("fence", it["n"], "ACT"))

            V = nc.vector

            def op(ins, *keys):
                ins.then_inc(vector_done, w.step(*keys))

            def unit(it):
                e, g = it["evac"], it["g"]
                kind = e[0]
                if kind in ("act", "glu_a"):
                    return
                if kind == "conv_in":
                    if e[1] == "Sigmoid":
                        u = e[2]
                        dve.wait_ge(scalar_done, w.at("evac", g))
                        cu = R["cu"][:, 2 * u:2 * u + 2, CONV_W - 1:PADT]
                        V.tensor_tensor(cu, cu, R["conv_gate"], ALU.mult).then_inc(vector_done, w.step(("conv_gate_used", g)))
                        w.mark("evac_all", g)
                    return
                if kind == "fir_a" or kind == "fir_b":
                    l, i = e[1], e[2]
                    b = 4 * (i % 2) + (2 if kind == "fir_b" else 0)
                    dve.wait_ge(scalar_done, w.at("fir_0", g))
                    for tap in (1, 0):
                        dve.wait_ge(vector_done, w.now())
                        d = 2 - tap
                        for j in range(2):
                            tile = (0 if kind == "fir_a" else 22) + 2 * i + j
                            o = R["fir"][:, b + j, d:T]
                            last = V.scalar_tensor_tensor(out=o, in0=gbank(it["bank"])[:, j, 0:T - d],
                                                          scalar=col(f"b{l}_fw", tap * 44 + tile), in1=o, op0=ALU.mult,
                                                          op1=ALU.add)
                            last.then_inc(vector_done, w.step())
                    w.mark("evac", g)
                    w.mark("fir_sum", g)
                    if kind == "fir_b":
                        dve.wait_ge(scalar_done, w.at("fir_silu", g))
                        dve.wait_ge(vector_done, w.now())
                        a = 4 * (i % 2)
                        V.tensor_tensor(R["hid"][:, 2 * i:2 * i + 2, :], R["fir"][:, a:a + 2, :],
                                           R["fir"][:, a + 2:a + 4, :], ALU.mult).then_inc(vector_done, w.step(("fir_used", g + 2), ("fir_used", g + 1)))
                    return
                dve.wait_ge(tensor_done, w.at("unit", g))
                ps = gbank(it["bank"])
                if kind == "glu_b":
                    i = e[1]
                    dve.wait_ge(scalar_done, w.at("glu_a", g - 1))
                    V.tensor_tensor(R["hid"][:, 2 * i:2 * i + 2, :], ps, R["silu"][:, 2 * (i % 2):2 * (i % 2) + 2, :],
                                       ALU.mult).then_inc(vector_done, w.step(("evac", g)))
                elif kind == "gate":
                    _, name, u, add = e
                    y, gate = R["h"][:, 2 * u:2 * u + 2, :], R[name][:, 2 * u:2 * u + 2, :]
                    if not add:
                        V.tensor_tensor(y, ps, gate, ALU.mult).then_inc(vector_done, w.step(("evac", g)))
                    else:
                        V.tensor_tensor(gate, ps, gate, ALU.mult).then_inc(vector_done, w.step(("evac", g)))
                        dve.wait_ge(vector_done, w.now())
                        V.tensor_tensor(y, y, gate, ALU.add).then_inc(vector_done, w.step())
                elif kind == "gate_bias":
                    _, name, u, bias = e
                    y, gate = R["h"][:, 2 * u:2 * u + 2, :], R[name][:, 2 * u:2 * u + 2, :]
                    for j in range(2):
                        V.scalar_tensor_tensor(out=gate[:, j, :], in0=ps[:, j, :], scalar=col(bias, 2 * u + j),
                                                  in1=gate[:, j, :], op0=ALU.add, op1=ALU.mult).then_inc(vector_done, w.step(("evac", g)))
                    dve.wait_ge(vector_done, w.now())
                    V.tensor_tensor(y, y, gate, ALU.add).then_inc(vector_done, w.step())
                elif kind == "resid":
                    _, layer, at, u = e
                    for j in range(2):
                        x = R["x"][:, 2 * u + j, :]
                        V.scalar_tensor_tensor(out=x, in0=ps[:, j, :],
                                                  scalar=ada[:, layer % 2, at + 2 * u + j:at + 2 * u + j + 1], in1=x,
                                                  op0=ALU.mult, op1=ALU.add).then_inc(vector_done, w.step(("evac", g)))

            def norm(it):
                begin(it)
                sq, t1, y, u = temps(it)
                nt, s = it["nt"], it["s"]
                dve.wait_ge(tensor_done, w.at("sums", s))
                nn = 1 if it["total"] else nt
                for b in range((nn + 1) // 2):
                    m = min(2, nn - 2 * b)
                    V.tensor_scalar(t1[:, 2 * b:2 * b + m, :],
                                       sbank(b)[:, 0:m * T].rearrange("p (a t) -> p a t", t=T), it["inv"], EPS, ALU.mult,
                                       ALU.add).then_inc(vector_done, w.step(("mean", s)))
                dve.wait_ge(scalar_done, w.at("root", s))
                yy, uu, tt = y[:, 0:nn, :], u[:, 0:nn, :], t1[:, 0:nn, :]
                V.tensor_tensor(uu, yy, yy, ALU.mult).then_inc(vector_done, w.step())
                dve.wait_ge(vector_done, w.now())
                V.tensor_tensor(uu, uu, tt, ALU.mult).then_inc(vector_done, w.step())
                dve.wait_ge(vector_done, w.now())
                V.tensor_scalar(uu, uu, -0.5 * it["const"], 1.5 * it["const"], ALU.mult, ALU.add).then_inc(vector_done, w.step())
                dve.wait_ge(vector_done, w.now())
                V.tensor_tensor(yy, yy, uu, ALU.mult).then_inc(vector_done, w.step())
                dve.wait_ge(vector_done, w.now())
                src, dst = R[it["src"]], R[it["dst"]]
                for t in range(nt):
                    if it["gain"] == "A":
                        gcol = acol[:, t:t + 1]
                    else:
                        gcol = col(it["gain"], t if colat[it["gain"]][1] > 1 else 0)
                    V.scalar_tensor_tensor(out=dst[:, t, :], in0=src[:, t, :], scalar=gcol,
                                              in1=y[:, 0 if it["total"] else t, :], op0=ALU.mult, op1=ALU.mult).then_inc(vector_done, w.step(("scaled_tile", s, t), ("scaled", s)))
                post = it["post"]
                if post and post[0] == "mul":
                    dve.wait_ge(vector_done, w.now())
                    V.tensor_tensor(dst[:, 0:nt, :], dst[:, 0:nt, :], R[post[1]][:, 0:nt, :], ALU.mult).then_inc(vector_done, w.step())
                if post and post[0] == "rope":
                    dve.wait_ge(vector_done, w.now())
                    d = dst[:, 0:nt, :]
                    cos = R["cos" + post[1]].to_broadcast([P, nt, T]) if nt > 1 else R["cos" + post[1]]
                    sin = R["sin" + post[1]].to_broadcast([P, nt, T]) if nt > 1 else R["sin" + post[1]]
                    dve.wait_ge(tensor_done, w.at("turned", s))
                    V.tensor_tensor(d, d, cos, ALU.mult).then_inc(vector_done, w.step())
                    for b in range((nt + 1) // 2):
                        m = min(2, nt - 2 * b)
                        V.tensor_tensor(t1[:, 2 * b:2 * b + m, :],
                                           sbank(2 + b)[:, 0:m * T].rearrange("p (a t) -> p a t", t=T),
                                           sin[:, 2 * b:2 * b + m, :] if nt > 1 else sin, ALU.mult).then_inc(vector_done, w.step())
                    dve.wait_ge(vector_done, w.now())
                    V.tensor_tensor(d, d, t1[:, 0:nt, :], ALU.add).then_inc(vector_done, w.step())

            def hg_prep(it):
                begin(it)
                s, z, e, qt = it["s"], R["z"], R["e"], R["qt"]
                if it["layer"] == 0:
                    V.scalar_tensor_tensor(out=e, in0=z, scalar=-1.0, in1=z, op0=ALU.mult, op1=ALU.max).then_inc(vector_done, w.step(("abs_z", s)))
                    dve.wait_ge(scalar_done, w.at("softplus", s))
                    V.scalar_tensor_tensor(out=qt, in0=z, scalar=0.0, in1=e, op0=ALU.min, op1=ALU.subtract).then_inc(vector_done, w.step())
                    dve.wait_ge(vector_done, w.now())
                else:
                    V.tensor_tensor(small[:, 8:12], col("a1_lb", 0, 4), col("a0_lb", 0, 4), ALU.subtract).then_inc(vector_done, w.step(("lb_in", s)))
                    dve.wait_ge(scalar_done, w.at("lb", s))
                    dve.wait_ge(scalar_done, w.at("kin", s))
                    V.tensor_scalar(small[:, 12:16], small[:, 8:12], -1.0, 1.0, ALU.mult, ALU.add).then_inc(vector_done, w.step())
                    dve.wait_ge(vector_done, w.now())
                    for h in range(4):
                        V.tensor_scalar(e[:, h, :], e[:, h, :], small[:, 12 + h:13 + h], small[:, 8 + h:9 + h],
                                           ALU.mult, ALU.add).then_inc(vector_done, w.step())
                        V.tensor_scalar(R["kin"][:, h, :], R["kin"][:, h, :], small[:, 12 + h:13 + h], None, ALU.mult).then_inc(vector_done, w.step())
                    dve.wait_ge(vector_done, w.now())
                    V.tensor_single_scalar(e, e, 2.0 ** -63, ALU.max).then_inc(vector_done, w.step(("forget", s)))
                    dve.wait_ge(scalar_done, w.at("log_f", s))
                for h in range(4):
                    V.tensor_tensor_scan(R["b"][:, h, :], con("ones"), qt[:, h, :], 0.0, ALU.mult, ALU.add).then_inc(vector_done, w.step())
                V.memset(R["sc"], 0.0).then_inc(vector_done, w.step())

            def hg_level(it):
                begin(it)
                n, s = it["level"], it["s"]
                flat = lambda name: R[name].rearrange("p a t -> p (a t)")
                sc = R["sc"]
                if n == 0:
                    w.mark("decayed", s)
                if n > 0:
                    b = flat("b").rearrange("p (m w) -> p m w", w=2 * n)
                    e = flat("e").rearrange("p (m w) -> p m w", w=2 * n)
                    ref = b[:, :, n - 1:n].to_broadcast([P, 4 * T // (2 * n), n])
                    V.tensor_tensor(e[:, :, 0:n], ref, b[:, :, 0:n], ALU.subtract).then_inc(vector_done, w.step())
                    V.tensor_tensor(e[:, :, n:2 * n], b[:, :, n:2 * n], ref, ALU.subtract).then_inc(vector_done, w.step(("spans", s)))
                    dve.wait_ge(scalar_done, w.at("decays", s))
                    V.tensor_tensor(R["qt"], R["q"], R["e"], ALU.mult).then_inc(vector_done, w.step())
                    V.tensor_tensor(R["kt"], R["kin"], R["e"], ALU.mult).then_inc(vector_done, w.step(("decayed", s)))
                dve.wait_ge(tensor_done, w.at("level", s))
                if n == 128:
                    V.tensor_copy(sc[:, 1, :], sbank(0)).then_inc(vector_done, w.step())
                else:
                    m = con("ident") if n == 0 else con("levels", P * LEVELS.index(n), P)
                    m = m.bitcast(I32).unsqueeze(1).to_broadcast([P, 4, P])
                    for t in range(2):
                        V.copy_predicated(sc[:, 2 * t, :].rearrange("p (h n) -> p h n", h=4), m,
                                             sbank(t).rearrange("p (h n) -> p h n", h=4)).then_inc(vector_done, w.step())

            def attn(it):
                begin(it)
                soft_s, soft_w, turned = soft(it)
                what, s = it["what"], it["s"]
                if it["out"]:
                    i, q = it["out"]
                    dve.wait_ge(tensor_done, w.at("attn_out", s))
                    dst = R[{"diff": "dq", "moba": "mq", "mla": "qn"}[what]][:, i, q * P:(q + 1) * P]
                    if what == "diff":
                        V.tensor_copy(dst, sbank(3)[:, 0:P]).then_inc(vector_done, w.step())
                    else:
                        V.tensor_copy(dst[0:64, :], sbank(3)[0:64, 0:P]).then_inc(vector_done, w.step())
                        V.tensor_copy(dst[64:128, :], sbank(3)[64:128, P:2 * P]).then_inc(vector_done, w.step())
                if it["load"]:
                    i, q = it["load"]
                    n = (q + 1) * P
                    k0 = T - n
                    dve.wait_ge(tensor_done, w.at("scores", s))
                    scale = {"diff": 64 ** -0.5, "moba": 64 ** -0.5, "mla": 96 ** -0.5}[what]
                    bias = con("alibi", T * i + k0, n) if what == "diff" else con("mask", k0, n)
                    V.scalar_tensor_tensor(out=soft_s[:, :, 0:n],
                                              in0=psum[:, GBANKS:GBANKS + 2, 0:n],
                                              scalar=scale, in1=bias.unsqueeze(1).to_broadcast([P, 2, n]),
                                              op0=ALU.mult, op1=ALU.add).then_inc(vector_done, w.step())
                    dve.wait_ge(vector_done, w.now())
                    V.tensor_reduce(small[:, 20:22], soft_s[:, :, 0:n], AX.X, ALU.max).then_inc(vector_done, w.step())
                    dve.wait_ge(vector_done, w.now())
                    V.tensor_single_scalar(small[:, 22:24], small[:, 20:22], -1.0, ALU.mult).then_inc(vector_done, w.step(("neg_max", s)))
                    dve.wait_ge(scalar_done, w.at("exps", s))
                    V.reciprocal(small[:, 26:28], small[:, 24:26]).then_inc(vector_done, w.step())
                    dve.wait_ge(vector_done, w.now())
                    dve.wait_ge(tensor_done, w.at("attn_turn", s))
                    if what == "diff":
                        V.tensor_scalar(small[:, 28:29], small[:, 27:28], small[:, 5:6], None, ALU.mult).then_inc(vector_done, w.step())
                        dve.wait_ge(vector_done, w.now())
                        V.tensor_scalar(soft_s[:, 1, 0:n], soft_s[:, 1, 0:n], small[:, 28:29], None, ALU.mult).then_inc(vector_done, w.step())
                        dve.wait_ge(vector_done, w.now())
                        V.scalar_tensor_tensor(out=soft_w[:, 0, 0:n], in0=soft_s[:, 0, 0:n], scalar=small[:, 26:27],
                                                  in1=soft_s[:, 1, 0:n], op0=ALU.mult, op1=ALU.add).then_inc(vector_done, w.step())
                    else:
                        for c in range(2):
                            V.tensor_scalar(soft_w[:, c, 0:n], soft_s[:, c, 0:n], small[:, 26 + c:27 + c], None,
                                               ALU.mult).then_inc(vector_done, w.step())

            def router(it):
                begin(it)
                s = it["s"]
                L = small[:, 48:64].rearrange("p (t e) -> p t e", t=2)
                E = small[:, 64:80].rearrange("p (t e) -> p t e", t=2)
                dve.wait_ge(tensor_done, w.at("logits", s))
                V.tensor_copy(L, sbank(0)[:, 0:16].rearrange("p (t e) -> p t e", t=2)).then_inc(vector_done, w.step())
                dve.wait_ge(vector_done, w.now())
                V.tensor_reduce(small[:, 80:82], L, AX.X, ALU.max).then_inc(vector_done, w.step())
                dve.wait_ge(vector_done, w.now())
                V.tensor_single_scalar(small[:, 82:84], small[:, 80:82], -1.0, ALU.mult).then_inc(vector_done, w.step(("neg_max", s)))
                big = work[:, hb + 2048:hb + 2048 + 256]
                gt = big[:, 0:128].rearrange("p (t e j) -> p t e j", t=2, e=8)
                eq = big[:, 128:256].rearrange("p (t e j) -> p t e j", t=2, e=8)
                for t in range(2):
                    lj = L[:, t, :].unsqueeze(1).to_broadcast([P, 8, 8])
                    le = L[:, t, :].unsqueeze(2).to_broadcast([P, 8, 8])
                    V.tensor_tensor(gt[:, t], lj, le, ALU.is_gt).then_inc(vector_done, w.step())
                    V.tensor_tensor(eq[:, t], lj, le, ALU.is_equal).then_inc(vector_done, w.step())
                dve.wait_ge(vector_done, w.now())
                for t in range(2):
                    V.tensor_tensor(eq[:, t], eq[:, t], con("before").rearrange("p (e j) -> p e j", e=8), ALU.mult).then_inc(vector_done, w.step())
                dve.wait_ge(vector_done, w.now())
                V.tensor_tensor(big[:, 0:128], big[:, 0:128], big[:, 128:256], ALU.add).then_inc(vector_done, w.step())
                dve.wait_ge(vector_done, w.now())
                for t in range(2):
                    V.tensor_reduce(small[:, 88 + 8 * t:96 + 8 * t], gt[:, t], AX.X, ALU.add).then_inc(vector_done, w.step())
                dve.wait_ge(vector_done, w.now())
                V.tensor_single_scalar(small[:, 88:104], small[:, 88:104], 2.0, ALU.is_lt).then_inc(
                    vector_done, w.step(("chosen", s)))
                dve.wait_ge(vector_done, w.now())
                dve.wait_ge(scalar_done, w.at("exps", s))
                V.tensor_tensor(small[:, 64:80], small[:, 64:80], small[:, 88:104], ALU.mult).then_inc(vector_done, w.step())
                dve.wait_ge(vector_done, w.now())
                V.tensor_reduce(small[:, 84:86], E, AX.X, ALU.add).then_inc(vector_done, w.step())
                dve.wait_ge(vector_done, w.now())
                V.reciprocal(small[:, 86:88], small[:, 84:86]).then_inc(vector_done, w.step())
                dve.wait_ge(vector_done, w.now())
                for t in range(2):
                    V.tensor_scalar(E[:, t, :], E[:, t, :], small[:, 86 + t:87 + t], None, ALU.mult).then_inc(vector_done, w.step())
                dve.wait_ge(vector_done, w.now())
                ro = route.rearrange("p (e f) -> p f e", f=4)
                dve.wait_ge(tensor_done, w.at("places", s))
                for t in range(2):
                    V.tensor_scalar(small[:, 104:112], small[:, 88 + 8 * t:96 + 8 * t], -1000.0, 1000.0, ALU.mult,
                                    ALU.add).then_inc(vector_done, w.step())
                    dve.wait_ge(vector_done, w.now())
                    V.tensor_tensor(ro[:, t, :], sbank(0)[:, 16 + 8 * t:24 + 8 * t], small[:, 104:112],
                                    ALU.add).then_inc(vector_done, w.step())
                    V.tensor_copy(ro[:, 2 + t, :], E[:, t, :]).then_inc(vector_done, w.step())
                    dve.wait_ge(vector_done, w.now())
                V.tensor_reduce(small[:, 148:149], sbank(0)[:, 32:40], AX.X, ALU.max).then_inc(
                    vector_done, w.step(("placed", s)))
                dve.wait_ge(vector_done, w.now())
                V.tensor_scalar(small[:, 149:150], small[:, 148:149], float(P), 1.0, ALU.is_gt, ALU.add).then_inc(
                    vector_done, w.step())
                dve.wait_ge(vector_done, w.now())
                V.tensor_copy(passes[:, :], small[:, 149:150]).then_inc(vector_done, w.step(("passes",)))
                dve.wait_ge(tensor_done, w.at("h_turned", s))
                for half in range(4):
                    t, q = half // 2, half % 2
                    V.tensor_copy(h_tok[:, t, q * 512:(q + 1) * 512], sbank((half + 1) % 4)).then_inc(
                        vector_done, w.step())

            def rope_tables(it):
                begin(it)
                s = it["s"]
                tmp = temps(it)[0]
                posf, turns, ang = tmp[:, 1, :], tmp[:, 2, :], tmp[:, 3, :]
                dve.wait_ge(inputs_loaded, w.at("inputs"))
                V.tensor_copy(posf, pos[:, :]).then_inc(vector_done, w.step())
                magic = 1.5 * 2.0 ** 23
                c1, c2 = 6.28125, float(np.float32(int(0.0019353071795864769 * 2 ** 21) / 2 ** 21))
                c3 = 2 * math.pi - c1 - c2
                for j, name in enumerate(("64", "32")):
                    dve.wait_ge(vector_done, w.now())
                    V.tensor_scalar(ang, posf, con("freq" + name), None, ALU.mult).then_inc(vector_done, w.step())
                    dve.wait_ge(vector_done, w.now())
                    V.tensor_scalar(turns, ang, 1.0 / (2 * math.pi), magic, ALU.mult, ALU.add).then_inc(vector_done, w.step())
                    dve.wait_ge(vector_done, w.now())
                    V.tensor_single_scalar(turns, turns, magic, ALU.subtract).then_inc(vector_done, w.step())
                    for c in (c1, c2, c3):
                        dve.wait_ge(vector_done, w.now())
                        V.scalar_tensor_tensor(out=ang, in0=turns, scalar=-c, in1=ang, op0=ALU.mult, op1=ALU.add).then_inc(vector_done, w.step())
                    dve.wait_ge(vector_done, w.now())
                    V.tensor_scalar(R["cos" + name][:, 0, :], ang, 3.1415925, -3.1415925, ALU.min, ALU.max).then_inc(vector_done, w.step(("angle", s, j)))
                    dve.wait_ge(scalar_done, w.at("half", s, j))
                    cos = R["cos" + name][:, 0, :]
                    V.tensor_tensor(cos, cos, cos, ALU.mult).then_inc(vector_done, w.step())
                    dve.wait_ge(vector_done, w.now())
                    V.tensor_scalar(cos, cos, -2.0, 1.0, ALU.mult, ALU.add).then_inc(vector_done, w.step())
                V.memset(R["cu"][:, :, 0:CONV_W - 1], 0.0).then_inc(vector_done, w.step())

            def expert(r, e):
                dve.wait_ge(vector_round, r.at("r_end", last_round=True))
                V.tensor_copy(now4, route[:, bass.ds(e * 4, 4)]).then_inc(vector_round, r.step(("r_now",)))
                dve.wait_ge(vector_round, r.now())
                dve.wait_ge(tensor_round, r.at("r_weights", last_round=True))
                for t in range(2):
                    V.tensor_scalar(pick[:, t, :], con("slots"), now4[:, t:t + 1], None, ALU.is_equal).then_inc(
                        vector_round, r.step(("r_pick",)))
                dve.wait_ge(vector_round, r.now())
                for t in range(2):
                    V.tensor_scalar(weigh[:, t, :], pick[:, t, :], now4[:, 2 + t:3 + t], None, ALU.mult).then_inc(
                        vector_round, r.step(("r_weigh",)))
                dve.wait_ge(tensor_round, r.at("r_weights"))
                dve.wait_ge(tensor_round, r.at("r_bank", ROUND_BANKS - 1, last_round=True))
                V.tensor_copy(back, sbank(2)[:, 0:T]).then_inc(vector_round, r.step(("r_back",)))
                for i in range(FE_U):
                    dve.wait_ge(scalar_round, r.at("r_silu", i))
                    dve.wait_ge(tensor_round, r.at("r_turn", i - 2) if i >= 2 else
                                r.at("r_turn", FE_U - 2 + i, last_round=True))
                    V.tensor_tensor(hid_s[:, i % 2, :], up_s[:, i % 2, :], psum[:, (2 + i) % GBANKS, T:2 * T],
                                    ALU.mult).then_inc(vector_round, r.step(("r_evac", 2 + i)))
                for u in range(4):
                    b = 4 + FE_U + u
                    dve.wait_ge(tensor_round, r.at("r_bank", b))
                    for j in range(2):
                        x = R["x"][:, 2 * u + j, :]
                        V.scalar_tensor_tensor(out=x, in0=psum[:, b % GBANKS, j * T:(j + 1) * T],
                                               scalar=ada[:, 1, 40 + 2 * u + j:41 + 2 * u + j], in1=x, op0=ALU.mult,
                                               op1=ALU.add).then_inc(vector_round, r.step(("r_evac", b), ("r_end",)))

            def run(steps):
                for it in steps:
                    kind = it["kind"]
                    if kind == "unit":
                        unit(it)
                    elif kind == "fence":
                        fence(it)
                    elif kind == "end":
                        pass
                    elif kind == "ada":
                        n = it["n"]
                        dve.wait_ge(tensor_done, w.at("ada_sum", n))
                        if n == 0:
                            dve.wait_ge(inputs_loaded, w.at("inputs"))
                        pre = ("a0", "a1", "b0", "b1")[it["layer"]]
                        V.tensor_tensor(ada[:, it["layer"] % 2, 2 * it["a"]:2 * it["a"] + 2], ada_bank[:, 0:2],
                                           col(pre + "_mod_b", 2 * it["a"], 2), ALU.add).then_inc(vector_done, w.step(("ada", n)))
                    else:
                        if kind == "norm":
                            norm(it)
                        elif kind == "modcols":
                            begin(it)
                            dve.wait_ge(vector_done, w.now())
                            sc = ada[:, it["layer"] % 2, it["scale"]:it["scale"] + 8]
                            V.scalar_tensor_tensor(out=acol[:, :], in0=sc, scalar=1.0, in1=col(it["gain"], 0, 8),
                                                      op0=ALU.add, op1=ALU.mult).then_inc(vector_done, w.step())
                            dve.wait_ge(vector_done, w.now())
                        elif kind == "hg_prep":
                            hg_prep(it)
                        elif kind == "hg_level":
                            hg_level(it)
                        elif kind == "attn":
                            attn(it)
                        elif kind == "lam":
                            begin(it)
                            l, s = it["layer"], it["s"]
                            lam = col(f"a{l}_lam", 0, 4).rearrange("p (a b) -> p a b", b=2)
                            V.tensor_tensor(small[:, 0:2], lam[:, :, 0], lam[:, :, 1], ALU.mult).then_inc(vector_done, w.step(("lam_products", s)))
                            dve.wait_ge(scalar_done, w.at("lam_exps", s))
                            V.tensor_tensor(small[:, 4:5], small[:, 3:4], small[:, 2:3], ALU.subtract).then_inc(vector_done, w.step())
                            dve.wait_ge(vector_done, w.now())
                            V.tensor_single_scalar(small[:, 5:6], small[:, 4:5], -LAM_INIT[l], ALU.add).then_inc(vector_done, w.step())
                            dve.wait_ge(vector_done, w.now())
                        elif kind == "conv":
                            begin(it)
                            t, l = it["tile"], it["layer"]
                            dve.wait_ge(vector_done, w.at("conv_gate_used", it["needs"][0][1]))
                            dve.wait_ge(vector_done, w.now())
                            y = R["ca"][:, t, :]
                            for tap in range(CONV_W):
                                u = R["cu"][:, t, tap:tap + T]
                                wcol = col(f"b{l}_dw_w", tap * 4 + t)
                                if tap == 0:
                                    V.tensor_scalar(y, u, wcol, col(f"b{l}_dw_b", t), ALU.mult, ALU.add).then_inc(vector_done, w.step())
                                else:
                                    V.scalar_tensor_tensor(out=y, in0=u, scalar=wcol, in1=y, op0=ALU.mult, op1=ALU.add).then_inc(vector_done, w.step())
                                dve.wait_ge(vector_done, w.now())
                        elif kind == "center":
                            begin(it)
                            dve.wait_ge(tensor_done, w.at("center", it["s"]))
                            mu = temps(it)[1][:, 0:1, :]
                            V.tensor_scalar(mu, sbank(0)[:, 0:T].unsqueeze(1), 1.0 / 512, None, ALU.mult).then_inc(vector_done, w.step())
                            dve.wait_ge(vector_done, w.now())
                            V.tensor_tensor(R["ca"], R["ca"], mu.to_broadcast([P, 4, T]), ALU.subtract).then_inc(vector_done, w.step())
                            dve.wait_ge(vector_done, w.now())
                        elif kind == "router":
                            router(it)
                        elif kind == "rope_tables":
                            rope_tables(it)
                        w.mark("side", it["s"], w.name)

            run(before)
            if after:
                dve.wait_ge(vector_done, w.at("passes"))
                n_passes = dve.value_load(passes[0:1, 0:1], min_val=1, max_val=2)
                dve.drain().then_inc(vector_round, Rounds("DVE", book, 0).share())
                with dve.Fori(0, n_passes) as p:
                    with dve.Fori(0, EXPERTS) as e:
                        expert(Rounds("DVE", book, p * EXPERTS + e), e)
                    r = Rounds("DVE", book, p * EXPERTS + EXPERTS - 1)
                    dve.wait_ge(vector_round, r.at("r_end"))
                    V.tensor_scalar(route.rearrange("p (e f) -> p e f", f=4)[:, :, 0:2],
                                    route.rearrange("p (e f) -> p e f", f=4)[:, :, 0:2], float(P), None,
                                    ALU.subtract).then_inc(vector_pass, 1)
                    dve.wait_ge(vector_pass, p + 1)
                dve.drain().then_inc(vector_done, w.step(("experts_over", "DVE")))
            run(after)

        @block.gpsimd
        def _(pool):
            w = Count("POOL", book)
            G = nc.gpsimd
            steps = [it for it in plan if it["kind"] == "ada"]

            def load(k):
                if k < len(steps):
                    it = steps[k]
                    pool.wait_ge(gpsimd_done, w.now())
                    pool.dma_start(mod_in[:, k % 2, :], arrays["mods"][it["layer"], it["a"]]).then_inc(
                        mod_loaded[k % 2], w.step(("mod_in", k), of=f"mod{k % 2}", by=16))

            load(0)
            load(1)
            pool.wait_ge(scalar_done, w.at("silu_c"))
            for k, it in enumerate(steps):
                buf = mod_in[:, k % 2, :]
                b3 = buf.rearrange("p (k n) -> p k n", k=DK)
                cvec = act_c[:, it["layer"] // 2, :].unsqueeze(2).to_broadcast([P, DK, 256])
                pool.wait_ge(mod_loaded[k % 2], w.at("mod_in", k))
                G.tensor_tensor(b3, b3, cvec, ALU.mult).then_inc(gpsimd_done, w.step())
                for h in (1024, 512):
                    pool.wait_ge(gpsimd_done, w.now())
                    G.tensor_tensor(buf[:, 0:h], buf[:, 0:h], buf[:, h:2 * h], ALU.add).then_inc(gpsimd_done, w.step())
                pool.wait_ge(gpsimd_done, w.now())
                if k >= ACCS:
                    pool.wait_ge(tensor_done, w.at("ada_sum", k - ACCS))
                G.tensor_tensor(mod_acc[:, k % ACCS, :], buf[:, 0:256], buf[:, 256:512], ALU.add).then_inc(gpsimd_done, w.step(("mod_acc", k)))
                load(k + 2)


def lay_out(i):
    def tiles(w, cols):
        k, n = w.shape
        return w.reshape(k // P, P, n // cols, cols).transpose(2, 1, 0, 3).reshape(n // cols, P, -1)

    def column(v):
        return v.reshape(-1, P).T

    def twice(v, n):
        return np.tile(v, n)[:, None]

    a = {}
    x = i["x"][0]
    a["xT"] = x.T.reshape(8, P, T).transpose(1, 0, 2)
    a["mods"] = np.stack([tiles(w, 256) for w in (*i["ada_w"], *i["w_mod_2"])])
    a["w_in1"] = np.stack([tiles(w, 512) for w in i["w_in"]])
    a["w_pa"] = np.stack([tiles(w, 1024)[0] for w in i["w_branch_a"]])
    a["w_pb"] = np.stack([tiles(w, 1024)[0] for w in i["w_branch_b"]])
    a["w_o1"] = np.stack([tiles(w, 512) for w in i["w_out"]])

    def pairs(w1, w3):
        n = w1.shape[1] // 256
        both = np.stack([w1.reshape(D, n, 256), w3.reshape(D, n, 256)], 2).reshape(D, n * 512)
        return tiles(both, 512)

    def halves(w):
        k, n = w.shape
        kt = k // P
        return w.reshape(2, kt // 2, P, 4, 256).transpose(3, 0, 2, 1, 4).reshape(4, 2, P, -1)

    a["f13"] = pairs(i["ffn_w1"][0], i["ffn_w3"][0])
    a["f2"] = halves(i["ffn_w2"][0])
    a["m13"] = np.stack([pairs(w1, w3) for w1, w3 in zip(i["moe_w1"][0], i["moe_w3"][0])])
    a["m2"] = i["moe_w2"][0].reshape(EXPERTS, 4, 7, P, 2, 512).transpose(0, 4, 1, 3, 2, 5).reshape(EXPERTS, 2, 4, P, -1)
    w = i["w_in_2"]
    lat = np.concatenate([w[:, :, :640], np.tile(w[:, :, 640:672], (1, 1, 4))], 2)
    main = np.concatenate([lat[:, :, :512], w[:, :, 672:]], 2)
    a["w_in2"] = np.stack([tiles(x, 512) for x in main])
    a["w_in2x"] = np.stack([tiles(np.ascontiguousarray(x[:, 512:]), 256)[0] for x in lat])
    uq = i["w_uq_2"].reshape(2, 384, 8, 96)
    a["w_uq"] = np.stack([tiles(np.concatenate([u[:, :, :64].reshape(384, 512), u[:, :, 64:].reshape(384, 256)], 1), 768)[0]
                          for u in uq])
    ukv = i["w_ukv_2"].reshape(2, 256, 8, 128)
    a["w_ukv"] = np.stack([tiles(np.concatenate([u[:, :, :64].reshape(256, 512), u[:, :, 64:].reshape(256, 512)], 1), 1024)[0]
                           for u in ukv])
    for name, key in (("w_mla", "w_mla_o_2"), ("w_moba", "w_moba_o_2"), ("w_pw", "w_conv_pw2_2")):
        a[name] = np.stack([tiles(w, 1024)[0] for w in i[key]])
    a["w_o2"] = np.stack([tiles(w, 512) for w in i["w_out_2"]])
    a["up"] = np.stack([pairs(w[:, :D_FF], w[:, D_FF:]) for w in i["w_up_2"]])
    a["down"] = np.stack([halves(w) for w in i["w_down_2"]])
    a["positions"] = i["positions_2"].reshape(1, T)
    at, n = column_map()
    c = np.zeros((P, n), np.float32)

    def put(name, value):
        o, wd = at[name]
        c[:, o:o + wd] = value

    put("c1", column(i["c"][0]))
    put("c2", column(i["c_2"][0]))
    for l in range(2):
        put(f"a{l}_mix_g", column(i["norm_mix_g"][l]))
        put(f"a{l}_ffn_g", column(i["norm_ffn_g"][l]))
        put(f"a{l}_lb", column(i["hgrn_lb_logits"][l]))
        put(f"a{l}_hg_g", column(i["hgrn_norm_g"][l]))
        put(f"a{l}_qn_g", twice(i["da_qnorm_g"][l], 2))
        put(f"a{l}_kn_g", twice(i["da_knorm_g"][l], 2))
        put(f"a{l}_lam", np.tile(i["da_lambda"][l].T, (2, 1)))
        put(f"a{l}_sub_g", column(i["da_subln_g"][l]))
        put(f"a{l}_mod_b", column(i["ada_b"][l]))
        put(f"b{l}_mix_g", column(i["mix_norm_g_2"][l]))
        put(f"b{l}_ffn_g", column(i["ffn_norm_g_2"][l]))
        put(f"b{l}_mod_b", column(i["b_mod_2"][l]))
        put(f"b{l}_ql_g", column(i["mla_q_norm_g_2"][l]))
        put(f"b{l}_kl_g", column(i["mla_kv_norm_g_2"][l]))
        put(f"b{l}_qn_g", twice(i["mla_qn_nope_g_2"][l], 2))
        put(f"b{l}_qr_g", twice(i["mla_qn_rope_g_2"][l], 4))
        put(f"b{l}_kn_g", twice(i["mla_kn_nope_g_2"][l], 2))
        put(f"b{l}_kr_g", twice(i["mla_kn_rope_g_2"][l], 4))
        put(f"b{l}_bq_g", twice(i["moba_qn_g_2"][l], 2))
        put(f"b{l}_bk_g", twice(i["moba_kn_g_2"][l], 2))
        put(f"b{l}_dw_w", i["conv_dw_w_2"][l].reshape(CONV_W, 4, P).transpose(2, 0, 1).reshape(P, -1))
        put(f"b{l}_dw_b", column(i["conv_dw_b_2"][l]))
        put(f"b{l}_ln_g", column(i["conv_ln_g_2"][l]))
        put(f"b{l}_ln_b", column(i["conv_ln_b_2"][l]))
        put(f"b{l}_pw_b", column(i["b_conv_pw2_2"][l]))
        put(f"b{l}_fw", i["ffn_dw_w_2"][l].reshape(3, 44, P).transpose(2, 0, 1).reshape(P, -1))
        put(f"b{l}_fb", column(i["ffn_dw_b_2"][l]))
    put("router", i["moe_router"][0].reshape(DK, P, 8).transpose(1, 0, 2).reshape(P, 64))
    a["columns"] = c
    a["constants"] = constants()
    return {k: np.ascontiguousarray(v) for k, v in a.items()}


def program(bacc, shapes, book):
    nc = bacc.Bacc("TRN2", target_bir_lowering=False, num_devices=1)
    aps = {k: nc.dram_tensor("in_" + k, s, d, kind="ExternalInput").ap() for k, (s, d) in shapes.items()}
    out = nc.dram_tensor("xT_out", (P, 8, T), F32, kind="ExternalOutput").ap()
    build(nc, aps, out, book, aps["columns"], aps["constants"])
    return nc


def kernel(**inputs):
    import concourse.bacc as bacc
    from concourse.bass_utils import run_bass_kernel_spmd
    arrays = lay_out({k: np.asarray(v) for k, v in inputs.items()})
    shapes = {k: (v.shape, mybir.dt.from_np(v.dtype)) for k, v in arrays.items()}
    book = Book()
    program(bacc, shapes, book)
    book.known, book.whole = book.at, book.count
    nc = program(bacc, shapes, book)
    r = run_bass_kernel_spmd(nc, [{"in_" + k: v for k, v in arrays.items()}], core_ids=[0])
    y = r.results[0]["xT_out"]
    return np.ascontiguousarray(y.transpose(2, 1, 0).reshape(1, T, D))
```
